# Optimizing a Trainium2 kernel written in Bass

```python
import math
import jax, jax.numpy as jnp
from jax import lax
import numpy as np

D_MODEL = 2048
BATCH = 1
SEQ = 256
DEPTH = 1

PLE_DIM = 256
ATTN_HEADS = 8
ATTN_HEAD_DIM = 128
ATTN_WIDTH = ATTN_HEADS * ATTN_HEAD_DIM
MOBA_BLOCK = 256
MOBA_TOPK = 3
MOBA_Q_BLOCK = 128
REL_BUCKETS = 32
REL_MAX_DISTANCE = 128
SSM_D_INNER = D_MODEL
SSM_HEAD_DIM = 64
SSM_HEADS = SSM_D_INNER // SSM_HEAD_DIM
SSM_GROUPS = 4
SSM_STATE = 128
SSM_CONV = 4
SSM_CHUNK = 256
SSM_CONV_DIM = SSM_D_INNER + 2 * SSM_GROUPS * SSM_STATE
SC_WIDTH = D_MODEL // 2
SC_CONV = 3
N_BRANCHES = 3
D_FF = 4 * D_MODEL
IN_PROJ_WIDTH = 3 * ATTN_WIDTH + SSM_D_INNER + SSM_CONV_DIM + SSM_HEADS + 3 * SC_WIDTH + N_BRANCHES * D_MODEL
NORM_EPS = 1e-6
NEG_INF = -1e30

kernel_name = "hybrid_moba_ssd_shortconv_trunk"

def rms_norm(x, g):
    xf = x.astype(jnp.float32)
    y = xf * lax.rsqrt(jnp.mean(xf * xf, axis=-1, keepdims=True) + NORM_EPS)
    return (y * g.astype(jnp.float32)).astype(x.dtype)

def causal_depthwise_conv(x, w):
    width, ch = w.shape
    return lax.conv_general_dilated(
        x, w[:, None, :].astype(x.dtype), window_strides=(1,), padding=[(width - 1, 0)],
        dimension_numbers=("NWC", "WIO", "NWC"), feature_group_count=ch)

def t5_bucket(rel):
    n = jnp.maximum(rel, 0)
    max_exact = REL_BUCKETS // 2
    nf = jnp.maximum(n, 1).astype(jnp.float32)
    large = max_exact + (jnp.log(nf / max_exact) / math.log(REL_MAX_DISTANCE / max_exact)
                         * (REL_BUCKETS - max_exact)).astype(jnp.int32)
    large = jnp.minimum(large, REL_BUCKETS - 1)
    return jnp.where(n < max_exact, n, large)

def moba_attention(q, k, v, rel_bias):
    b, s, h, dh = q.shape
    s_pad = -(-s // MOBA_BLOCK) * MOBA_BLOCK
    pad = ((0, 0), (0, s_pad - s), (0, 0), (0, 0))
    q, k, v = [jnp.pad(t, pad).transpose(0, 2, 1, 3) for t in (q, k, v)]
    nb = s_pad // MOBA_BLOCK
    topk = min(MOBA_TOPK, nb)
    k_blk = k.reshape(b, h, nb, MOBA_BLOCK, dh)
    v_blk = v.reshape(b, h, nb, MOBA_BLOCK, dh)
    k_mean = jnp.mean(k_blk.astype(jnp.float32), axis=3)
    table_h = rel_bias.T.astype(jnp.float32)
    bidx = jnp.arange(b)[:, None, None, None]
    hidx = jnp.arange(h)[None, :, None, None]
    scale = dh ** -0.5
    blk_ar = jnp.arange(MOBA_BLOCK)

    def query_block(c):
        start = c * MOBA_Q_BLOCK
        q_c = lax.dynamic_slice_in_dim(q, start, MOBA_Q_BLOCK, axis=2)
        q_pos = start + jnp.arange(MOBA_Q_BLOCK)
        qblk = start // MOBA_BLOCK
        gate = jnp.einsum("bhqd,bhnd->bhqn", q_c.astype(jnp.float32), k_mean)
        gate = jnp.where(jnp.arange(nb) < qblk, gate, -jnp.inf)
        _, sel = lax.top_k(gate, topk)
        valid = sel < qblk
        k_sel = k_blk[bidx, hidx, sel]
        v_sel = v_blk[bidx, hidx, sel]
        k_pos = sel[..., None] * MOBA_BLOCK + blk_ar
        bias_sel = table_h[hidx[..., None], t5_bucket(q_pos[:, None, None] - k_pos)]
        s_sel = jnp.einsum("bhqd,bhqkld->bhqkl", q_c, k_sel).astype(jnp.float32) * scale + bias_sel
        s_sel = jnp.where(valid[..., None], s_sel, NEG_INF)
        k_own = lax.dynamic_index_in_dim(k_blk, qblk, axis=2, keepdims=False)
        v_own = lax.dynamic_index_in_dim(v_blk, qblk, axis=2, keepdims=False)
        rel_own = q_pos[:, None] - (qblk * MOBA_BLOCK + blk_ar)[None, :]
        bias_own = table_h[:, t5_bucket(rel_own)]
        s_own = jnp.einsum("bhqd,bhld->bhql", q_c, k_own).astype(jnp.float32) * scale + bias_own
        s_own = jnp.where(rel_own >= 0, s_own, NEG_INF)
        logits = jnp.concatenate(
            [s_sel.reshape(b, h, MOBA_Q_BLOCK, topk * MOBA_BLOCK), s_own], axis=-1)
        probs = jax.nn.softmax(logits, axis=-1).astype(v.dtype)
        p_sel = probs[..., :topk * MOBA_BLOCK].reshape(b, h, MOBA_Q_BLOCK, topk, MOBA_BLOCK)
        p_own = probs[..., topk * MOBA_BLOCK:]
        return (jnp.einsum("bhqkl,bhqkld->bhqd", p_sel, v_sel)
                + jnp.einsum("bhql,bhld->bhqd", p_own, v_own))

    outs = lax.map(query_block, jnp.arange(s_pad // MOBA_Q_BLOCK))
    return outs.transpose(1, 0, 3, 2, 4).reshape(b, s_pad, h * dh)[:, :s]

def ssd_chunked(x, dt, a_head, bmat, cmat):
    b, s, h, p = x.shape
    g, n = bmat.shape[2], bmat.shape[3]
    e = h // g
    s_pad = -(-s // SSM_CHUNK) * SSM_CHUNK
    ps = s_pad - s
    x = jnp.pad(x, ((0, 0), (0, ps), (0, 0), (0, 0)))
    dt = jnp.pad(dt, ((0, 0), (0, ps), (0, 0)))
    bmat = jnp.pad(bmat, ((0, 0), (0, ps), (0, 0), (0, 0)))
    cmat = jnp.pad(cmat, ((0, 0), (0, ps), (0, 0), (0, 0)))
    c, L = s_pad // SSM_CHUNK, SSM_CHUNK
    xdt = (x * dt[..., None]).reshape(b, c, L, g, e, p)
    a = (dt * a_head).reshape(b, c, L, g, e).transpose(0, 3, 4, 1, 2)
    bm = bmat.reshape(b, c, L, g, n)
    cm = cmat.reshape(b, c, L, g, n)
    a_cum = jnp.cumsum(a, axis=-1)
    causal = jnp.tril(jnp.ones((L, L), dtype=bool))
    seg = a_cum[..., :, None] - a_cum[..., None, :]
    decay_in = jnp.exp(jnp.where(causal, seg, -jnp.inf))
    cb = jnp.einsum("bclgn,bcsgn->bgcls", cm, bm)
    y_diag = jnp.einsum("bgcls,bgecls,bcsgep->bclgep", cb, decay_in, xdt)
    decay_states = jnp.exp(a_cum[..., -1:] - a_cum)
    states = jnp.einsum("bclgn,bgecl,bclgep->bcgepn", bm, decay_states, xdt)
    chunk_decay = jnp.exp(a_cum[..., -1])

    def step(hstate, inp):
        st, dc = inp
        return hstate * dc[..., None, None] + st, hstate

    h0 = jnp.zeros((b, g, e, p, n), dtype=x.dtype)
    _, prev = lax.scan(step, h0, (states.transpose(1, 0, 2, 3, 4, 5), chunk_decay.transpose(3, 0, 1, 2)))
    prev = prev.transpose(1, 0, 2, 3, 4, 5)
    y_off = jnp.einsum("bclgn,bcgepn,bgecl->bclgep", cm, prev, jnp.exp(a_cum))
    return (y_diag + y_off).reshape(b, s_pad, h, p)[:, :s]

def mamba2_mixer(z, xbc, dt_raw, conv_w, conv_b, dt_bias, a_log, d_skip, norm_g):
    b, s, _ = z.shape
    xbc = jax.nn.silu(causal_depthwise_conv(xbc, conv_w) + conv_b.astype(xbc.dtype))
    gn = SSM_GROUPS * SSM_STATE
    xs, bm, cm = jnp.split(xbc, [SSM_D_INNER, SSM_D_INNER + gn], axis=-1)
    xs_h = xs.reshape(b, s, SSM_HEADS, SSM_HEAD_DIM).astype(jnp.float32)
    dt = jax.nn.softplus(dt_raw.astype(jnp.float32) + dt_bias.astype(jnp.float32))
    a_head = -jnp.exp(a_log.astype(jnp.float32))
    y = ssd_chunked(xs_h, dt, a_head,
                    bm.reshape(b, s, SSM_GROUPS, SSM_STATE).astype(jnp.float32),
                    cm.reshape(b, s, SSM_GROUPS, SSM_STATE).astype(jnp.float32))
    y = y + d_skip.astype(jnp.float32)[:, None] * xs_h
    y = y.reshape(b, s, SSM_D_INNER) * jax.nn.silu(z.astype(jnp.float32))
    yg = y.reshape(b, s, SSM_GROUPS, SSM_D_INNER // SSM_GROUPS)
    yg = yg * lax.rsqrt(jnp.mean(yg * yg, axis=-1, keepdims=True) + NORM_EPS)
    return (yg.reshape(b, s, SSM_D_INNER) * norm_g.astype(jnp.float32)).astype(z.dtype)

def setup_inputs(seed: int = 0) -> dict:
    key = jax.random.key(seed)
    ks = jax.random.split(key, 32)

    def w(k, fan_in, fan_out):
        return jax.random.normal(k, (DEPTH, fan_in, fan_out), jnp.float32) * fan_in ** -0.5

    def gain(k, width):
        return 1.0 + 0.05 * jax.random.normal(k, (DEPTH, width), jnp.float32)

    u = jax.random.uniform(ks[8], (DEPTH, SSM_HEADS), jnp.float32)
    dt0 = jnp.exp(u * (math.log(0.1) - math.log(0.001)) + math.log(0.001))
    return {
        "x": jax.random.normal(ks[0], (BATCH, SEQ, D_MODEL), jnp.float32),
        "p": jax.random.normal(ks[1], (DEPTH, BATCH, SEQ, PLE_DIM), jnp.float32),
        "rel_bias": 0.5 * jax.random.normal(ks[2], (REL_BUCKETS, ATTN_HEADS), jnp.float32),
        "g_mix_pre": gain(ks[3], D_MODEL),
        "w_in": w(ks[4], D_MODEL, IN_PROJ_WIDTH),
        "ssm_conv_w": jax.random.normal(ks[5], (DEPTH, SSM_CONV, SSM_CONV_DIM), jnp.float32) * SSM_CONV ** -0.5,
        "ssm_conv_b": 0.01 * jax.random.normal(ks[6], (DEPTH, SSM_CONV_DIM), jnp.float32),
        "ssm_dt_bias": dt0 + jnp.log(-jnp.expm1(-dt0)),
        "ssm_a_log": jnp.log(jax.random.uniform(ks[9], (DEPTH, SSM_HEADS), jnp.float32, 1.0, 16.0)),
        "ssm_d": 1.0 + 0.1 * jax.random.normal(ks[10], (DEPTH, SSM_HEADS), jnp.float32),
        "ssm_norm_g": gain(ks[11], SSM_D_INNER),
        "sc_conv_w": jax.random.normal(ks[12], (DEPTH, SC_CONV, SC_WIDTH), jnp.float32) * SC_CONV ** -0.5,
        "w_br_attn": w(ks[13], ATTN_WIDTH, D_MODEL),
        "w_br_ssm": w(ks[14], SSM_D_INNER, D_MODEL),
        "w_br_conv": w(ks[15], SC_WIDTH, D_MODEL),
        "w_out": w(ks[16], D_MODEL, D_MODEL),
        "g_mix_post": gain(ks[17], D_MODEL),
        "g_mlp_pre": gain(ks[18], D_MODEL),
        "w_mlp_up": w(ks[19], D_MODEL, D_FF),
        "w_mlp_down": w(ks[20], D_FF, D_MODEL),
        "g_mlp_post": gain(ks[21], D_MODEL),
        "g_ple_pre": gain(ks[22], D_MODEL),
        "w_ple_gate": w(ks[23], D_MODEL, D_MODEL),
        "w_ple_proj": w(ks[24], PLE_DIM, D_MODEL),
        "g_ple_post": gain(ks[25], D_MODEL),
    }

def reference(x, p, rel_bias, g_mix_pre, w_in, ssm_conv_w, ssm_conv_b, ssm_dt_bias, ssm_a_log,
              ssm_d, ssm_norm_g, sc_conv_w, w_br_attn, w_br_ssm, w_br_conv, w_out, g_mix_post,
              g_mlp_pre, w_mlp_up, w_mlp_down, g_mlp_post, g_ple_pre, w_ple_gate, w_ple_proj,
              g_ple_post):
    b, s, _ = x.shape
    sizes = (ATTN_WIDTH, ATTN_WIDTH, ATTN_WIDTH, SSM_D_INNER, SSM_CONV_DIM, SSM_HEADS,
             SC_WIDTH, SC_WIDTH, SC_WIDTH, N_BRANCHES * D_MODEL)
    offsets = [int(o) for o in np.cumsum(sizes)[:-1]]
    for i in range(DEPTH):
        h = rms_norm(x, g_mix_pre[i])
        proj = jnp.einsum("bsd,de->bse", h, w_in[i])
        q, k, v, z, xbc, dt_raw, sc_b, sc_c, sc_h, gates = jnp.split(proj, offsets, axis=-1)
        y_attn = moba_attention(q.reshape(b, s, ATTN_HEADS, ATTN_HEAD_DIM),
                                k.reshape(b, s, ATTN_HEADS, ATTN_HEAD_DIM),
                                v.reshape(b, s, ATTN_HEADS, ATTN_HEAD_DIM), rel_bias)
        y_ssm = mamba2_mixer(z, xbc, dt_raw, ssm_conv_w[i], ssm_conv_b[i], ssm_dt_bias[i],
                             ssm_a_log[i], ssm_d[i], ssm_norm_g[i])
        y_sc = sc_b * causal_depthwise_conv(sc_c * sc_h, sc_conv_w[i])
        g_a, g_m, g_c = jnp.split(jax.nn.sigmoid(gates), N_BRANCHES, axis=-1)
        merged = (g_a * jnp.einsum("bse,ed->bsd", y_attn, w_br_attn[i])
                  + g_m * jnp.einsum("bse,ed->bsd", y_ssm, w_br_ssm[i])
                  + g_c * jnp.einsum("bse,ed->bsd", y_sc, w_br_conv[i]))
        x = x + rms_norm(jnp.einsum("bsd,de->bse", merged, w_out[i]), g_mix_post[i])
        hm = rms_norm(x, g_mlp_pre[i])
        u = jnp.square(jax.nn.relu(jnp.einsum("bsd,df->bsf", hm, w_mlp_up[i])))
        x = x + rms_norm(jnp.einsum("bsf,fd->bsd", u, w_mlp_down[i]), g_mlp_post[i])
        gate = jax.nn.sigmoid(jnp.einsum("bsd,de->bse", rms_norm(x, g_ple_pre[i]), w_ple_gate[i]))
        emb = jnp.einsum("bsk,kd->bsd", p[i].astype(x.dtype), w_ple_proj[i])
        x = x + rms_norm(gate * emb, g_ple_post[i])
    return x


_drawn_inputs = setup_inputs


def setup_inputs(seed=0):
    import zlib

    import numpy as np

    out = dict(_drawn_inputs(seed))
    spreads = {}
    factors = {'ssm_conv_b': 8.0, 'g_ple_pre': 5.77}
    for name, (base, spread) in spreads.items():
        noise = np.random.default_rng([zlib.crc32(name.encode()), seed]).standard_normal(out[name].shape)
        drawn = base * np.exp(spread * noise) if base else spread * noise
        out[name] = __import__('jax').numpy.asarray(drawn.astype(out[name].dtype))
    for name, factor in factors.items():
        out[name] = (out[name] * factor).astype(out[name].dtype)
    return out
```

```python
from contextlib import ExitStack

import numpy as np

import concourse.bass as bass
from concourse import mybir

F32 = mybir.dt.float32
F32R = mybir.dt.float32r
ALU = mybir.AluOpType
ACT = mybir.ActivationFunctionType
AX = mybir.AxisListType
ds = bass.ds

P = 128
T = 256
D = 2048
DT = D // P
HEADS, BUCKETS = 8, 32
GROUPS, GROUP_HEADS, HEAD_DIM = 4, 8, 64
SSM_HEADS = GROUPS * GROUP_HEADS
EPS = 1e-6
MASKED = -1e30
CAUSAL = T + P

SLOTS = 4
LEAD = SLOTS - 1
BLOCK = 4

STAGES = [
    ("qkv", 48, 12),
    ("att", 64, 16),
    ("dt", 2, 1),
    ("ga", 48, 16),
    ("gc", 48, 16),
    ("xs", 8, 2),
    ("ssd", 64, 16),
    ("gm", 56, 14),
    ("emb", 4, 8),
    ("out", 32, 8),
    ("mlp", 256, 64),
    ("ple", 32, 8),
]
UNIT0, BLOCK0 = {}, {}
_u = _b = 0
for _name, _units, _blocks in STAGES:
    UNIT0[_name], BLOCK0[_name] = _u, _b
    _u, _b = _u + _units, _b + _blocks
UNITS = _u

G_MIX_PRE, G_MIX_POST, G_MLP_PRE, G_MLP_POST, G_PLE_PRE, G_PLE_POST, G_SSM, D_SKIP = (
    DT * i for i in range(8))
CONV_W = 8 * DT
CONV_B = CONV_W + 24 * 4
SC_W = CONV_B + 24
CONSTS = SC_W + 8 * 3


def bucket_starts():
    n = np.arange(T)
    nf = np.maximum(n, 1).astype(np.float32)
    half = BUCKETS // 2
    large = half + (np.log(nf / np.float32(half)) / np.float32(np.log(128 / half))
                    * np.float32(BUCKETS - half)).astype(np.int32)
    bucket = np.where(n < half, n, np.minimum(large, BUCKETS - 1))
    return [int(np.searchsorted(bucket, b)) for b in range(BUCKETS)] + [T]


def build(nc, wstream, x_in, p_in, consts_in, heads_in, rel_in, out):
    bias_rows = nc.dram_tensor("bias_rows", [HEADS, P, CAUSAL], F32)
    decay_rows = nc.dram_tensor("decay_rows", [SSM_HEADS, T], F32)

    at = [(nc.sbuf_base + 63) // 64 * 64]

    def place(name, shape, dt=F32, where=None):
        size = 4 * int(np.prod(shape[1:]))
        if where is None:
            where = at[0]
            at[0] += (size + 31) // 32 * 32
        return nc.alloc_sbuf_tensor_at(name, shape, dt, offset=where)

    def region(kib):
        where = at[0]
        at[0] += kib * 1024
        return where

    raw = place("w_raw", [P, SLOTS, 1024])
    whi = place("w_hi", [P, SLOTS, 1024], F32R)
    wlo = place("w_lo", [P, SLOTS, 1024], F32R)
    xT = place("x_T", [P, DT, T])
    act1 = place("act1", [P, DT, 2, T], F32R)
    right = place("right", [P, 2, 2, T])
    ev = place("ev", [P, 2, 2, T])
    sq = place("sq", [P, 2 * T])
    sq_sum = place("sq_sum", [P, 2 * T])
    rs = place("rs", [P, T])
    rg = place("rg", [P, T])
    consts = place("consts", [P, CONSTS])
    ident = place("ident", [P, P])
    ones = place("ones", [P, P])
    pT = place("p_T", [P, 2, T])
    p_act = place("p_act", [P, 2, 2, T], F32R)
    dt_raw = place("dt_raw", [SSM_HEADS, T])
    head_consts = place("head_consts", [SSM_HEADS, 2])
    w1 = region(16)
    merged = place("merged", [P, DT, T], where=w1)
    bias = place("bias", [P, HEADS, T], where=w1)
    att = place("att", [P, CAUSAL], where=w1 + 8192)
    attT = place("att_T", [P, CAUSAL], where=w1 + 9728)
    q_h = place("q_h", [P, T], where=w1 + 11264)
    v_h = place("v_h", [P, T], where=w1 + 12288)
    v_tok = place("v_tok", [P, 2, P], where=w1 + 13312)
    negmax = place("negmax", [P, 2], where=w1 + 14336)
    denom = place("denom", [P, 2], where=w1 + 14368)
    w2 = region(32)
    qkv = place("qkv", [P, 24, T], where=w2)
    y_sc = place("y_sc", [P, 8, 2, T], F32R, where=w2)
    act2 = place("act2", [P, DT, 2, T], F32R, where=w2)
    w3 = region(48)
    y_att = place("y_att", [P, 8, 2, T], F32R, where=w3)
    conv = place("conv", [P, 32, T], where=w3 + 16384)
    bc = place("bc", [P, 8, T], where=w3 + 16384)
    cb = place("cb", [P, GROUPS, CAUSAL], where=w3)
    a_rows = place("a_rows", [P, GROUP_HEADS, T], where=w3 + 6144)
    dtv = place("dt", [SSM_HEADS, T], where=w3 + 14336)
    a_cum = place("a_cum", [SSM_HEADS, T], where=w3 + 15360)
    t0 = w3 + 16384 + 8192
    decay = place("decay", [P, 4, CAUSAL], where=t0)
    group_sq = place("group_sq", [P, 4, T], where=t0)
    xs = place("xs", [P, 4, T], where=t0 + 6144)
    z = place("z", [P, 4, T], where=t0 + 10240)
    xdt = place("xdt", [P, 2, 512], where=t0 + 14336)
    mask = place("mask", [P, CAUSAL], where=t0 + 18432)
    dt_tok = place("dt_tok", [P, 2, SSM_HEADS], where=t0 + 19968)
    a_tok = place("a_tok", [P, 2, SSM_HEADS], where=t0 + 20224)
    s_abs = place("s_abs", [SSM_HEADS, T], where=t0)
    s_exp = place("s_exp", [SSM_HEADS, T], where=t0 + 1024)
    s_log = place("s_log", [SSM_HEADS, T], where=t0 + 2048)
    s_dif = place("s_dif", [SSM_HEADS, T], where=t0 + 3072)
    s_one = place("s_one", [SSM_HEADS, T], where=t0 + 4096)
    s_a = place("s_a", [SSM_HEADS, T], where=t0 + 5120)
    ah = place("ah", [SSM_HEADS, 1], where=t0 + 20480)
    act3 = place("act3", [P, DT, 2, T], F32R, where=w3)
    emb = place("emb", [P, DT, T], where=w3 + 32768)
    rel = place("rel", [HEADS, BUCKETS], where=w3)
    bias_row = place("bias_row", [HEADS, CAUSAL], where=w3 + 1024)
    assert at[0] <= nc.sbuf_usable_end, at[0]

    ctx = ExitStack()
    with ctx:
        def sem(name):
            return ctx.enter_context(nc.semaphore(name))

        ps = ctx.enter_context(nc.psum_tensor("ps", [P, 8, 512], F32))
        pair = [ps[:, 2 * g:2 * g + 2, :] for g in range(2)]
        bank = [ps[:, i, :] for i in range(8)]

        w_loaded = [sem(f"w_loaded{s}") for s in range(SLOTS)]
        hi_ready, lo_ready, unit_done = sem("hi_ready"), sem("lo_ready"), sem("unit_done")
        right_copied, block_done = sem("right_copied"), sem("block_done")
        x_loaded, p_loaded, consts_loaded = sem("x_loaded"), sem("p_loaded"), sem("consts_loaded")
        heads_loaded, rel_loaded = sem("heads_loaded"), sem("rel_loaded")
        made, ident_made, mask_made = sem("made"), sem("ident_made"), sem("mask_made")
        bias_filled, bias_stored, bias_loaded = sem("bias_filled"), sem("bias_stored"), sem("bias_loaded")
        sq_ready, sq_added, sumsq_done = sem("sq_ready"), sem("sq_added"), sem("sumsq_done")
        var_ready, std_ready, rs_ready = sem("var_ready"), sem("std_ready"), sem("rs_ready")
        normed, normed_hi, normed_lo = sem("normed"), sem("normed_hi"), sem("normed_lo")
        o_normed, x_updated = sem("o_normed"), sem("x_updated")
        head_staged, scores_done = sem("head_staged"), sem("scores_done")
        logits_ready, negmax_ready, exp_ready = sem("logits_ready"), sem("negmax_ready"), sem("exp_ready")
        denom_inv, probs_ready, probsT_done = sem("denom_inv"), sem("probs_ready"), sem("probsT_done")
        probsT_copied, v_tok_ready = sem("probsT_copied"), sem("v_tok_ready")
        pv_done, y_att_hi = sem("pv_done"), sem("y_att_hi")
        sc_product, sc_taps, sc_gated, sc_hi = sem("sc_product"), sem("sc_taps"), sem("sc_gated"), sem("sc_hi")
        gate_ready, branch_summed, branch_gated = sem("gate_ready"), sem("branch_summed"), sem("branch_gated")
        merged_hi = sem("merged_hi")
        dt_summed, bc_taps, bc_ready, cb_done, cb_masked = (
            sem("dt_summed"), sem("bc_taps"), sem("bc_ready"), sem("cb_done"), sem("cb_masked"))
        soft_dve, soft_act = sem("soft_dve"), sem("soft_act")
        a_ready, a_stored, tok_done, tok_copied = sem("a_ready"), sem("a_stored"), sem("tok_done"), sem("tok_copied")
        a_rows_loaded = [sem("a_rows_loaded0"), sem("a_rows_loaded1")]
        seg_ready, decay_ready, mix_ready = sem("seg_ready"), sem("decay_ready"), sem("mix_ready")
        xs_taps, xs_ready, xsT_done, xdt_ready = sem("xs_taps"), sem("xs_ready"), sem("xsT_done"), sem("xdt_ready")
        y_done, z_ready, y_skipped, y_gated = sem("y_done"), sem("z_ready"), sem("y_skipped"), sem("y_gated")
        group_squared, group_summed = sem("group_squared"), sem("group_summed")
        group_var, group_std, group_rs = sem("group_var"), sem("group_std"), sem("group_rs")
        y_normed, y_ssm_hi = sem("y_normed"), sem("y_ssm_hi")
        p_hi, p_split = sem("p_hi"), sem("p_split")
        up_summed, hidden_hi, down_summed = sem("up_summed"), sem("hidden_hi"), sem("down_summed")
        merged_zero, ple_summed, ple_gate, out_stored = (
            sem("merged_zero"), sem("ple_summed"), sem("ple_gate"), sem("out_stored"))

        block = ctx.enter_context(nc.Block())

        def two(tensor, i):
            return tensor[:, ds(2 * i, 2)]


        @block.sync
        def _(sp):
            for n in range(SLOTS):
                sp.dma_start(raw[:, n, :], wstream[n]).then_inc(w_loaded[n], 16)
            with sp.Fori(1, UNITS // SLOTS) as it:
                for s in range(SLOTS):
                    sp.wait_ge(lo_ready, it * SLOTS + (s + 1 - SLOTS))
                    sp.dma_start(raw[:, s, :], wstream[ds(it * SLOTS + s, 1)]
                                 .rearrange("o p n -> (o p) n")).then_inc(w_loaded[s], 16)
            for n in range(UNITS // SLOTS * SLOTS, UNITS):
                sp.wait_ge(lo_ready, n + 1 - SLOTS)
                sp.dma_start(raw[:, n % SLOTS, :], wstream[n]).then_inc(w_loaded[n % SLOTS], 16)
            for b in range(8):
                sp.wait_ge(x_updated, 16 + b + 1)
                sp.dma_start(out[:, 2 * b:2 * b + 2], xT[:, 2 * b:2 * b + 2]).then_inc(out_stored, 16)
            sp.wait_ge(out_stored, 8 * 16)

        @block.scalar
        def _(act):
            def split_hi(e, c):
                s = c % SLOTS
                act.wait_ge(w_loaded[s], e * 4 + 16 * (c // SLOTS + 1))
                if c >= SLOTS or not isinstance(e, int):
                    act.wait_ge(unit_done, e + (c + 1 - SLOTS))
                act.activation(whi[:, s, :], raw[:, s, :], ACT.Copy).then_inc(hi_ready, 1)

            def step(e, c):
                if isinstance(e, int) and e + c + LEAD >= UNITS:
                    return
                split_hi(e, c + LEAD)

            def copy_right(ue, uc, be, bc_):
                g = bc_ % 2
                act.wait_ge(unit_done, ue + (uc + 1))
                if bc_ >= 2 or not isinstance(be, int):
                    act.wait_ge(block_done, be + (bc_ - 1))
                act.activation(right[:, g], pair[g][:, :, T:2 * T], ACT.Copy).then_inc(right_copied, 1)

            def square(p, src):
                if p >= 1:
                    act.wait_ge(sq_added, p)
                act.activation(sq[:, :], src, ACT.Square).then_inc(sq_ready, 1)

            def std(r):
                act.wait_ge(var_ready, r + 1)
                act.activation(rs[:, :], rs[:, :], ACT.Sqrt).then_inc(std_ready, 1)

            def split_normed(k):
                for b in range(8):
                    act.wait_ge(normed, 8 * k + b + 1)
                    act.activation(act1[:, 2 * b:2 * b + 2, 0, :], ev[:, b % 2], ACT.Copy)\
                       .then_inc(normed_hi, 1)

            def sigmoid_gate(slot, be, bc_):
                act.wait_ge(block_done, be + (bc_ + 1))
                act.activation(ev[:, slot], ev[:, slot], ACT.Sigmoid).then_inc(gate_ready, 1)

            act.dma_start(xT[:, :, :], x_in).then_inc(x_loaded, 16)
            act.dma_start(consts[:, :], consts_in).then_inc(consts_loaded, 16)
            act.dma_start(rel[:, :], rel_in).then_inc(rel_loaded, 16)
            act.dma_start(head_consts[:, :], heads_in).then_inc(heads_loaded, 16)
            act.dma_start(pT[:, :, :], p_in).then_inc(p_loaded, 16)
            act.wait_ge(x_loaded, 16)
            for b in range(8):
                square(b, xT[:, 2 * b:2 * b + 2])
            for n in range(LEAD):
                split_hi(0, n)
            std(0)
            split_normed(0)

            def qkv_blocks(ue, be):
                for c in range(8):
                    step(ue, c)
                    if c % 4 == 3:
                        copy_right(ue, c, be, c // 4)

            qkv_blocks(0, 0)
            with act.Fori(1, 6) as it:
                qkv_blocks(it * 8, it * 2)

            U, B = UNIT0["att"], BLOCK0["att"]
            with act.Fori(0, 8) as h:
                for c in range(8):
                    step(h * 8, U + c)
                    if c == 0:
                        act.wait_ge(scores_done, h + 1)
                        act.activation(v_tok[:, :, :], bank[5][:, 0:T].rearrange("p (k d) -> p k d", k=2),
                                       ACT.Copy).then_inc(v_tok_ready, 1)
                    if c == 1:
                        act.wait_ge(negmax_ready, h + 1)
                        act.activation(att[:, 0:P], att[:, 0:P], ACT.Exp, bias=negmax[:, 0:1],
                                       accum_out=denom[:, 0:1])
                        act.activation(att[:, P:CAUSAL], att[:, P:CAUSAL], ACT.Exp, bias=negmax[:, 1:2],
                                       accum_out=denom[:, 1:2]).then_inc(exp_ready, 1)
                    if c == 6:
                        act.wait_ge(pv_done, h + 1)
                        act.activation(y_att[:, ds(h, 1), 0, :], bank[7][:, 0:T], ACT.Copy)\
                           .then_inc(y_att_hi, 1)
                    if c % 4 == 3:
                        copy_right(h * 8, U + c, h * 2, B + c // 4)

            U, B = UNIT0["dt"], BLOCK0["dt"]
            step(0, U)
            step(0, U + 1)
            act.wait_ge(unit_done, U + 2)
            act.wait_ge(block_done, B - 1)
            act.activation(right[0:SSM_HEADS, B % 2, 0, :], bank[2 * (B % 2)][0:SSM_HEADS, T:2 * T],
                           ACT.Copy).then_inc(right_copied, 1)

            for name in ("ga", "gc"):
                U, B = UNIT0[name], BLOCK0[name]
                with act.Fori(0, 4) as it:
                    for c in range(12):
                        step(it * 12, U + c)
                        if c in (3, 5, 9, 11):
                            copy_right(it * 12, U + c, it * 4, B + (3, 5, 9, 11).index(c))
                        if c in (4, 10):
                            sigmoid_gate(c // 10, it * 4, B + 2 * (c // 10))
                        if c == 7 and name == "ga":
                            act.wait_ge(sc_gated, it + 1)
                            act.activation(y_sc[:, ds(it * 2, 2), 0, :], conv[:, ds(it * 2 + 8, 2), :],
                                           ACT.Copy).then_inc(sc_hi, 1)

            U, B = UNIT0["xs"], BLOCK0["xs"]
            for c in range(8):
                step(0, U + c)
                if c == 0:
                    act.wait_ge(bc_taps, 16)
                    act.activation(bc[:, :, :], bc[:, :, :], ACT.Silu).then_inc(bc_ready, 1)
                if c == 1:
                    act.wait_ge(soft_dve, 1)
                    act.activation(s_exp[:, :], s_abs[:, :], ACT.Exp).then_inc(soft_act, 1)
                    act.activation(ah[:, :], head_consts[:, 1:2], ACT.Exp).then_inc(soft_act, 1)
                    act.wait_ge(soft_dve, 2)
                    act.activation(s_log[:, :], s_one[:, :], ACT.Ln).then_inc(soft_act, 1)
                if c % 4 == 3:
                    copy_right(0, U + c, 0, B + c // 4)

            U, B = UNIT0["ssd"], BLOCK0["ssd"]
            with act.Fori(0, GROUPS) as g:
                for c in range(16):
                    step(g * 16, U + c)
                    if c % 4 == 3:
                        copy_right(g * 16, U + c, g * 4, B + c // 4)
                    if c in (0, 8):
                        act.wait_ge(seg_ready, g * 2 + (c // 8 + 1))
                        act.activation(decay[:, :, :], decay[:, :, :], ACT.Exp).then_inc(decay_ready, 1)
                    if c == 4:
                        act.wait_ge(xs_taps, g * 4 + 4)
                        act.activation(xs[:, :, :], xs[:, :, :], ACT.Silu).then_inc(xs_ready, 1)
                    if c == 9:
                        act.wait_ge(block_done, g * 4 + (B + 2))
                        act.activation(z[:, :, :], z[:, :, :], ACT.Silu).then_inc(z_ready, 1)
                    if c == 12:
                        act.wait_ge(y_gated, g + 1)
                        act.activation(group_sq[:, :, :], xs[:, :, :], ACT.Square).then_inc(group_squared, 1)
                    if c == 14:
                        act.wait_ge(group_var, g + 1)
                        act.activation(rg[:, :], rg[:, :], ACT.Sqrt).then_inc(group_std, 1)
                    if c == 15:
                        act.wait_ge(y_normed, g + 1)
                        act.activation(act2[:, ds(g * 4, 4), 0, :], xs[:, :, :], ACT.Copy)\
                           .then_inc(y_ssm_hi, 1)

            U, B = UNIT0["gm"], BLOCK0["gm"]

            def split_merged(e, u, be, bc_):
                act.wait_ge(block_done, be + (bc_ + 1))
                act.activation(act3[:, ds(e + 2 * u, 2), 0, :], merged[:, ds(e + 2 * u, 2), :], ACT.Copy)\
                   .then_inc(merged_hi, 1)

            def branch_pair(ue, uc, be, bc_, e):
                for c in range(8):
                    step(ue, uc + c)
                    if c % 4 == 3:
                        copy_right(ue, uc + c, be, bc_ + c // 4)
                        split_merged(e, c // 4, be, bc_ + c // 4)

            for slot in range(2):
                sigmoid_gate(slot, 0, B - 2 + slot)
            with act.Fori(0, 3) as it:
                branch_pair(it * 16, U, it * 4, B, it * 4)
                for c in range(8, 16):
                    step(it * 16, U + c)
                    if c % 4 == 3:
                        copy_right(it * 16, U + c, it * 4, B + c // 4)
                    if c == 12:
                        sigmoid_gate(0, it * 4, B + 2)
                sigmoid_gate(1, it * 4, B + 3)
            branch_pair(0, U + 48, 0, B + 12, 12)

            U, B = UNIT0["emb"], BLOCK0["emb"]
            act.wait_ge(p_loaded, 16)
            act.activation(p_act[:, :, 0, :], pT[:, :, :], ACT.Copy).then_inc(p_hi, 1)
            for c in range(4):
                step(0, U + c)
                copy_right(0, U + c, 0, B + 2 * c)
                copy_right(0, U + c, 0, B + 2 * c + 1)

            U, B = UNIT0["out"], BLOCK0["out"]
            for b in range(8):
                for c in range(4):
                    step(0, U + 4 * b + c)
                copy_right(0, U + 4 * b + 3, 0, B + b)
                act.wait_ge(block_done, B + b + 1)
                square(8 + b, merged[:, 2 * b:2 * b + 2])
            std(1)
            for b in range(8):
                act.wait_ge(x_updated, b + 1)
                square(16 + b, xT[:, 2 * b:2 * b + 2])
            std(2)
            split_normed(1)

            def quarter(e, be, last):
                for b in range(8):
                    for c in range(4):
                        step(e, UNIT0["mlp"] + 4 * b + c)
                    copy_right(e, UNIT0["mlp"] + 4 * b + 3, be, BLOCK0["mlp"] + b)
                    act.wait_ge(block_done, be + (BLOCK0["mlp"] + b + 1))
                    act.activation(act2[:, 2 * b:2 * b + 2, 0, :], ev[:, b % 2], ACT.Copy)\
                       .then_inc(hidden_hi, 1)
                for b in range(8, 16):
                    for c in range(4):
                        step(e, UNIT0["mlp"] + 4 * b + c)
                    copy_right(e, UNIT0["mlp"] + 4 * b + 3, be, BLOCK0["mlp"] + b)
                    if last:
                        act.wait_ge(block_done, be + BLOCK0["mlp"] + b + 1)
                        square(24 + b - 8, merged[:, 2 * (b - 8):2 * (b - 8) + 2])

            with act.Fori(0, 3) as it:
                quarter(it * 64, it * 16, False)
            quarter(192, 48, True)
            std(3)
            for b in range(8):
                act.wait_ge(x_updated, 8 + b + 1)
                square(32 + b, xT[:, 2 * b:2 * b + 2])
            std(4)
            split_normed(2)

            U, B = UNIT0["ple"], BLOCK0["ple"]
            for b in range(8):
                for c in range(4):
                    step(0, U + 4 * b + c)
                copy_right(0, U + 4 * b + 3, 0, B + b)
                act.wait_ge(ple_summed, b + 1)
                act.activation(ev[:, b % 2], ev[:, b % 2], ACT.Sigmoid).then_inc(ple_gate, 1)
                act.wait_ge(block_done, B + b + 1)
                square(40 + b, merged[:, 2 * b:2 * b + 2])
            std(5)

        @block.vector
        def _(dve):
            def split_lo(e, c):
                s = c % SLOTS
                dve.wait_ge(hi_ready, e + (c + 1))
                dve.tensor_tensor(wlo[:, s, :], raw[:, s, :], whi[:, s, :], ALU.subtract)\
                   .then_inc(lo_ready, 1)

            def step(e, c):
                if isinstance(e, int) and e + c + LEAD >= UNITS:
                    return
                split_lo(e, c + LEAD)

            def sum_to(dst, be, bc_, signal):
                g = bc_ % 2
                dve.wait_ge(right_copied, be + (bc_ + 1))
                dve.tensor_tensor(dst, pair[g][:, :, 0:T], right[:, g], ALU.add).then_inc(signal, 1)

            def column(i):
                return consts[:, ds(i, 1)]

            def inv_rms(r):
                dve.wait_ge(sumsq_done, r + 1)
                dve.tensor_scalar(rs[:, :], bank[4][:, 0:T], 1.0 / D, EPS, ALU.mult, ALU.add)\
                   .then_inc(var_ready, 1)
                dve.wait_ge(std_ready, r + 1)
                dve.reciprocal(rs[:, :], rs[:, :]).then_inc(rs_ready, 1)
                dve.wait_ge(rs_ready, r + 1)

            def norm_x(k, gain):
                def low(b):
                    dve.wait_ge(normed_hi, 8 * k + b + 1)
                    dve.tensor_tensor(act1[:, 2 * b:2 * b + 2, 1, :], ev[:, b % 2],
                                      act1[:, 2 * b:2 * b + 2, 0, :], ALU.subtract).then_inc(normed_lo, 1)

                for b in range(8):
                    if b >= 2:
                        dve.wait_ge(normed_lo, 8 * k + b - 1)
                    for t in range(2):
                        i = dve.scalar_tensor_tensor(
                            ev[:, b % 2, t, :], xT[:, 2 * b + t, :], consts[:, gain + 2 * b + t:gain + 2 * b + t + 1],
                            rs[:, :], ALU.mult, ALU.mult)
                    i.then_inc(normed, 1)
                    if b >= 1:
                        low(b - 1)
                low(7)

            def add_normed(k, gain):
                for b in range(8):
                    for t in range(2):
                        i = dve.scalar_tensor_tensor(
                            merged[:, 2 * b + t, :], merged[:, 2 * b + t, :],
                            consts[:, gain + 2 * b + t:gain + 2 * b + t + 1], rs[:, :], ALU.mult, ALU.mult)
                    i.then_inc(o_normed, 1)
                    dve.wait_ge(o_normed, 8 * k + b + 1)
                    dve.tensor_tensor(xT[:, 2 * b:2 * b + 2], xT[:, 2 * b:2 * b + 2],
                                      merged[:, 2 * b:2 * b + 2], ALU.add).then_inc(x_updated, 1)

            for n in range(LEAD):
                split_lo(0, n)
            dve.wait_ge(x_loaded, 16)
            dve.wait_ge(consts_loaded, 16)
            inv_rms(0)
            norm_x(0, G_MIX_PRE)

            U, B = UNIT0["qkv"], BLOCK0["qkv"]
            with dve.Fori(0, 6) as it:
                for c in range(8):
                    step(it * 8, U + c)
                    if c % 4 == 3:
                        sum_to(qkv[:, ds(it * 4 + 2 * (c // 4), 2), :], it * 2, B + c // 4, block_done)

            U, B = UNIT0["att"], BLOCK0["att"]
            dve.wait_ge(bias_loaded, 16)
            with dve.Fori(0, 8) as h:
                for c in range(8):
                    step(h * 8, U + c)
                    if c == 0:
                        dve.wait_ge(scores_done, h + 1)
                        scale = float(P) ** -0.5
                        dve.scalar_tensor_tensor(att[:, 0:P], bank[4][:, 0:P], scale,
                                                 bias[:, ds(h, 1), P:T], ALU.mult, ALU.add)
                        dve.scalar_tensor_tensor(att[:, P:CAUSAL], bank[4][:, P:CAUSAL], scale,
                                                 bias[:, ds(h, 1), 0:T], ALU.mult, ALU.add)\
                           .then_inc(logits_ready, 1)
                        dve.wait_ge(logits_ready, h + 1)
                        dve.tensor_reduce(negmax[:, 0:1], att[:, 0:P], AX.X, ALU.max, negate=True)
                        dve.tensor_reduce(negmax[:, 1:2], att[:, P:CAUSAL], AX.X, ALU.max, negate=True)\
                           .then_inc(negmax_ready, 1)
                    if c == 2:
                        dve.wait_ge(exp_ready, h + 1)
                        dve.reciprocal(denom[:, :], denom[:, :]).then_inc(denom_inv, 1)
                        dve.wait_ge(denom_inv, h + 1)
                        dve.tensor_scalar(att[:, 0:P], att[:, 0:P], denom[:, 0:1], None, ALU.mult)
                        dve.tensor_scalar(att[:, P:CAUSAL], att[:, P:CAUSAL], denom[:, 1:2], None, ALU.mult)\
                           .then_inc(probs_ready, 1)
                    if c == 4:
                        dve.wait_ge(probsT_done, h + 1)
                        dve.tensor_copy(attT[:, :], bank[6][:, 0:CAUSAL]).then_inc(probsT_copied, 1)
                    if c == 6:
                        dve.wait_ge(y_att_hi, h + 1)
                        dve.tensor_tensor(y_att[:, ds(h, 1), 1, :], bank[7][:, 0:T],
                                          y_att[:, ds(h, 1), 0, :], ALU.subtract)
                    if c % 4 == 3:
                        sum_to(conv[:, ds(h * 4 + 2 * (c // 4), 2), :], h * 2, B + c // 4, block_done)

            U, B = UNIT0["dt"], BLOCK0["dt"]
            step(0, U)
            step(0, U + 1)
            dve.wait_ge(right_copied, B + 1)
            dve.wait_ge(heads_loaded, 16)
            dve.scalar_tensor_tensor(dt_raw[:, :], bank[2 * (B % 2)][0:SSM_HEADS, 0:T], head_consts[:, 0:1],
                                     right[0:SSM_HEADS, B % 2, 0, :], ALU.add, ALU.add).then_inc(block_done, 1)

            def gate_branch(be, bc_, slot, merge, m, first):
                g = bc_ % 2
                sum_to(right[:, g], be, bc_, branch_summed)
                dve.wait_ge(branch_summed, merge)
                dve.wait_ge(gate_ready, merge)
                if first:
                    dve.tensor_tensor(merged[:, ds(m, 2), :], right[:, g], ev[:, slot], ALU.mult)\
                       .then_inc(block_done, 1)
                    return
                dve.tensor_tensor(right[:, g], right[:, g], ev[:, slot], ALU.mult).then_inc(branch_gated, 1)
                dve.wait_ge(branch_gated, merge - 8)
                dve.tensor_tensor(merged[:, ds(m, 2), :], merged[:, ds(m, 2), :], right[:, g], ALU.add)\
                   .then_inc(block_done, 1)

            def sc_step(it, c):
                ch = conv[:, ds(it * 2, 2), :]
                y = conv[:, ds(it * 2 + 8, 2), :]

                def tap(k, shift):
                    for t in range(2):
                        w = column(it * 6 + (SC_W + 3 * t + k))
                        src = conv[:, ds(it * 2 + t, 1), 0:T - shift]
                        dst = conv[:, ds(it * 2 + (8 + t), 1), shift:T]
                        if shift == 0:
                            i = dve.tensor_scalar(dst, src, w, None, ALU.mult)
                        else:
                            i = dve.scalar_tensor_tensor(dst, src, w, dst, ALU.mult, ALU.add)
                    i.then_inc(sc_taps, 1)

                if c == 0:
                    dve.tensor_tensor(ch, ch, y, ALU.mult).then_inc(sc_product, 1)
                if c == 1:
                    dve.wait_ge(sc_product, it + 1)
                    tap(2, 0)
                if c == 2:
                    dve.wait_ge(sc_taps, it * 3 + 1)
                    tap(1, 1)
                if c == 4:
                    dve.wait_ge(sc_taps, it * 3 + 2)
                    tap(0, 2)
                if c == 6:
                    dve.wait_ge(sc_taps, it * 3 + 3)
                    dve.tensor_tensor(y, y, conv[:, ds(it * 2 + 16, 2), :], ALU.mult).then_inc(sc_gated, 1)
                if c == 8:
                    dve.wait_ge(sc_hi, it + 1)
                    dve.tensor_tensor(y_sc[:, ds(it * 2, 2), 1, :], y, y_sc[:, ds(it * 2, 2), 0, :],
                                      ALU.subtract)

            def conv4(src, dst, tile, k, signal):
                shift = 3 - k
                w, b = column(tile * 4 + (CONV_W + k)), column(tile + CONV_B)
                if shift == 0:
                    i = dve.tensor_scalar(dst(0, T), src(0, T), w, b, ALU.mult, ALU.add)
                else:
                    i = dve.scalar_tensor_tensor(dst(shift, T), src(0, T - shift), w, dst(shift, T),
                                                 ALU.mult, ALU.add)
                if signal is not None:
                    i.then_inc(signal, 1)

            def bc_step(it, c):
                if c not in (0, 1, 2, 4):
                    return
                k = {0: 3, 1: 2, 2: 1, 4: 0}[c]
                if c:
                    dve.wait_ge(bc_taps, it * 4 + (3 - k))
                for t in range(2):
                    conv4(lambda a, b: conv[:, ds(it * 2 + (24 + t), 1), a:b],
                          lambda a, b: bc[:, ds(it * 2 + t, 1), a:b], it * 2 + (16 + t), k,
                          bc_taps if t else None)

            for i, (name, side) in enumerate((("ga", sc_step), ("gc", bc_step))):
                U, B = UNIT0[name], BLOCK0[name]
                with dve.Fori(0, 4) as it:
                    for c in range(12):
                        step(it * 12, U + c)
                        side(it, c)
                        if c in (3, 9):
                            sum_to(ev[:, c // 9], it * 4, B + 2 * (c // 9), block_done)
                        if c in (5, 11):
                            gate_branch(it * 4, B + 1 + 2 * (c // 11), c // 11, it * 2 + (8 * i + c // 11 + 1),
                                        it * 4 + 2 * (c // 11), first=i == 0)

            U, B = UNIT0["xs"], BLOCK0["xs"]
            for c in range(8):
                step(0, U + c)
                if c == 0:
                    dve.scalar_tensor_tensor(s_abs[:, :], dt_raw[:, :], -1.0, dt_raw[:, :], ALU.mult, ALU.min)\
                       .then_inc(soft_dve, 1)
                if c == 1:
                    dve.wait_ge(soft_act, 2)
                    dve.tensor_scalar(s_one[:, :], s_exp[:, :], 1.0, None, ALU.add).then_inc(soft_dve, 1)
                    dve.wait_ge(soft_dve, 2)
                    dve.tensor_scalar(s_dif[:, :], s_one[:, :], -1.0, None, ALU.add).then_inc(soft_dve, 1)
                    dve.wait_ge(soft_dve, 3)
                    dve.tensor_scalar(s_a[:, :], s_dif[:, :], 0.0, None, ALU.is_equal).then_inc(soft_dve, 1)
                    dve.wait_ge(soft_dve, 4)
                    dve.tensor_tensor(s_dif[:, :], s_dif[:, :], s_a[:, :], ALU.add).then_inc(soft_dve, 1)
                    dve.wait_ge(soft_act, 3)
                    dve.tensor_tensor(s_log[:, :], s_log[:, :], s_a[:, :], ALU.add).then_inc(soft_dve, 1)
                    dve.wait_ge(soft_dve, 6)
                    dve.reciprocal(s_dif[:, :], s_dif[:, :]).then_inc(soft_dve, 1)
                    dve.tensor_tensor(s_log[:, :], s_log[:, :], s_exp[:, :], ALU.mult).then_inc(soft_dve, 1)
                    dve.wait_ge(soft_dve, 8)
                    dve.tensor_tensor(s_log[:, :], s_log[:, :], s_dif[:, :], ALU.mult).then_inc(soft_dve, 1)
                    dve.wait_ge(soft_dve, 9)
                    dve.scalar_tensor_tensor(dtv[:, :], dt_raw[:, :], 0.0, s_log[:, :], ALU.max, ALU.add)\
                       .then_inc(soft_dve, 1)
                    dve.memset(s_one[:, :], 1.0).then_inc(soft_dve, 1)
                    dve.wait_ge(soft_dve, 11)
                    dve.tensor_scalar(s_a[:, :], dtv[:, :], ah[:, 0:1], -1.0, ALU.mult, ALU.mult)\
                       .then_inc(soft_dve, 1)
                    dve.wait_ge(soft_dve, 12)
                    dve.tensor_tensor_scan(a_cum[:, :], s_one[:, :], s_a[:, :], 0.0, ALU.mult, ALU.add)\
                       .then_inc(a_ready, 1)
                if c == 3:
                    dve.wait_ge(mask_made, 3)
                    for g in range(GROUPS):
                        dve.wait_ge(cb_done, g + 1)
                        dve.tensor_tensor(cb[:, g, :], bank[4 + g][:, 0:CAUSAL], mask[:, :], ALU.mult)\
                           .then_inc(cb_masked, 1)
                if c == 6:
                    dve.wait_ge(tok_done, 1)
                    dve.tensor_copy(dt_tok[:, :, :], bank[4][:, 0:64].rearrange("p (k h) -> p k h", k=2))
                    dve.tensor_copy(a_tok[:, :, :], bank[4][:, 64:128].rearrange("p (k h) -> p k h", k=2))\
                       .then_inc(tok_copied, 1)
                if c % 4 == 3:
                    sum_to(ev[:, c // 4], 0, B + c // 4, block_done)

            U, B = UNIT0["ssd"], BLOCK0["ssd"]
            dve.wait_ge(tok_copied, 1)
            with dve.Fori(0, GROUPS) as g:
                def segments(half):
                    dve.wait_ge(a_rows_loaded[half], g * 16 + 16)
                    for i in range(4):
                        h = 4 * half + i
                        dve.tensor_scalar(decay[:, i, 0:T], a_rows[:, h, :], a_tok[:, 0, ds(g * 8 + h, 1)],
                                          0.0, ALU.subtract, ALU.min)
                        ins = dve.tensor_scalar(decay[:, i, T:CAUSAL], a_rows[:, h, P:T],
                                                a_tok[:, 1, ds(g * 8 + h, 1)], 0.0, ALU.subtract, ALU.min)
                    ins.then_inc(seg_ready, 1)

                def mix(half):
                    dve.wait_ge(decay_ready, g * 2 + (half + 1))
                    dve.tensor_tensor(decay[:, :, :], decay[:, :, :],
                                      cb[:, ds(g, 1), :].to_broadcast([P, 4, CAUSAL]), ALU.mult)\
                       .then_inc(mix_ready, 1)

                def taps(k):
                    for t in range(4):
                        conv4(lambda a, b: ev[:, t // 2, t % 2, a:b], lambda a, b: xs[:, t, a:b],
                              g * 4 + t, k, xs_taps if t == 3 else None)

                for c in range(16):
                    step(g * 16, U + c)
                    if c == 0:
                        segments(0)
                        dve.wait_ge(block_done, g * 4 + B)
                        dve.wait_ge(lo_ready, g * 16 + (U + 1 + LEAD))
                        taps(3)
                    if c == 1:
                        dve.wait_ge(xs_taps, g * 4 + 1)
                        taps(2)
                        mix(0)
                    if c == 2:
                        dve.wait_ge(xs_taps, g * 4 + 2)
                        taps(1)
                    if c == 3:
                        dve.wait_ge(xs_taps, g * 4 + 3)
                        taps(0)
                    if c == 5:
                        dve.wait_ge(xsT_done, g + 1)
                        for k in range(2):
                            ins = dve.tensor_tensor(
                                xdt[:, k, :].rearrange("p (h d) -> p h d", d=HEAD_DIM),
                                bank[4 + k].rearrange("p (h d) -> p h d", d=HEAD_DIM),
                                dt_tok[:, k, ds(g * 8, 8)].unsqueeze(2).to_broadcast([P, 8, HEAD_DIM]),
                                ALU.mult)
                        ins.then_inc(xdt_ready, 1)
                    if c in (3, 7):
                        sum_to(z[:, 2 * (c // 4):2 * (c // 4) + 2, :], g * 4, B + c // 4, block_done)
                    if c in (11, 15):
                        sum_to(ev[:, c // 4 - 2], g * 4, B + c // 4, block_done)
                    if c == 7:
                        dve.wait_ge(y_done, g * 2 + 1)
                        segments(1)
                    if c == 9:
                        mix(1)
                    if c == 11:
                        dve.wait_ge(y_done, g * 2 + 2)
                        for t in range(4):
                            ins = dve.scalar_tensor_tensor(
                                xs[:, t, :], xs[:, t, :], column(g * 4 + (D_SKIP + t)),
                                bank[6 + t // 2][:, t % 2 * T:t % 2 * T + T], ALU.mult, ALU.add)
                        ins.then_inc(y_skipped, 1)
                        dve.wait_ge(y_skipped, g + 1)
                        dve.wait_ge(z_ready, g + 1)
                        dve.tensor_tensor(xs[:, :, :], xs[:, :, :], z[:, :, :], ALU.mult).then_inc(y_gated, 1)
                    if c == 14:
                        dve.wait_ge(group_summed, g + 1)
                        dve.tensor_scalar(rg[:, :], bank[4][:, 0:T], 1.0 / 512, EPS, ALU.mult, ALU.add)\
                           .then_inc(group_var, 1)
                    if c == 15:
                        dve.wait_ge(group_std, g + 1)
                        dve.reciprocal(rg[:, :], rg[:, :]).then_inc(group_rs, 1)
                        dve.wait_ge(group_rs, g + 1)
                        for t in range(4):
                            ins = dve.scalar_tensor_tensor(xs[:, t, :], xs[:, t, :], column(g * 4 + (G_SSM + t)),
                                                           rg[:, :], ALU.mult, ALU.mult)
                        ins.then_inc(y_normed, 1)
                        dve.wait_ge(y_ssm_hi, g + 1)
                        dve.tensor_tensor(act2[:, ds(g * 4, 4), 1, :], xs[:, :, :], act2[:, ds(g * 4, 4), 0, :],
                                          ALU.subtract)

            U, B = UNIT0["gm"], BLOCK0["gm"]

            def branch_pair(ue, uc, be, bc_, e, merge):
                for c in range(8):
                    step(ue, uc + c)
                    if c % 4 == 3:
                        u = c // 4
                        gate_branch(be, bc_ + u, u, merge + (u + 1), e + 2 * u, first=False)
                        dve.wait_ge(merged_hi, merge + (u + 1 - 16))
                        dve.tensor_tensor(act3[:, ds(e + 2 * u, 2), 1, :], merged[:, ds(e + 2 * u, 2), :],
                                          act3[:, ds(e + 2 * u, 2), 0, :], ALU.subtract)

            with dve.Fori(0, 3) as it:
                branch_pair(it * 16, U, it * 4, B, it * 4, it * 2 + 16)
                for c in range(8, 16):
                    step(it * 16, U + c)
                    if c % 4 == 3:
                        sum_to(ev[:, c // 4 - 2], it * 4, B + c // 4, block_done)
            branch_pair(0, U + 48, 0, B + 12, 12, 22)

            U, B = UNIT0["emb"], BLOCK0["emb"]
            dve.wait_ge(p_hi, 1)
            dve.tensor_tensor(p_act[:, :, 1, :], pT[:, :, :], p_act[:, :, 0, :], ALU.subtract).then_inc(p_split, 1)
            for c in range(4):
                step(0, U + c)
                for b in (2 * c, 2 * c + 1):
                    sum_to(emb[:, 2 * b:2 * b + 2], 0, B + b, block_done)

            U, B = UNIT0["out"], BLOCK0["out"]
            for b in range(8):
                for c in range(4):
                    step(0, U + 4 * b + c)
                sum_to(merged[:, 2 * b:2 * b + 2], 0, B + b, block_done)
            inv_rms(1)
            add_normed(0, G_MIX_POST)
            inv_rms(2)
            norm_x(1, G_MLP_PRE)
            dve.memset(merged[:, :, :], 0.0).then_inc(merged_zero, 1)

            def quarter(e, be, qe):
                for b in range(8):
                    for c in range(4):
                        step(e, UNIT0["mlp"] + 4 * b + c)
                    sum_to(ev[:, b % 2], be, BLOCK0["mlp"] + b, up_summed)
                    dve.wait_ge(up_summed, qe + (b + 1))
                    dve.scalar_tensor_tensor(ev[:, b % 2], ev[:, b % 2], 0.0, ev[:, b % 2], ALU.max, ALU.mult)\
                       .then_inc(block_done, 1)
                    dve.wait_ge(hidden_hi, qe + (b + 1))
                    dve.tensor_tensor(act2[:, 2 * b:2 * b + 2, 1, :], ev[:, b % 2],
                                      act2[:, 2 * b:2 * b + 2, 0, :], ALU.subtract)
                for b in range(8, 16):
                    for c in range(4):
                        step(e, UNIT0["mlp"] + 4 * b + c)
                    g = (BLOCK0["mlp"] + b) % 2
                    sum_to(right[:, g], be, BLOCK0["mlp"] + b, down_summed)
                    dve.wait_ge(down_summed, qe + (b - 7))
                    y = merged[:, 2 * (b - 8):2 * (b - 8) + 2]
                    dve.tensor_tensor(y, y, right[:, g], ALU.add).then_inc(block_done, 1)

            dve.wait_ge(merged_zero, 1)
            with dve.Fori(0, 3) as it:
                quarter(it * 64, it * 16, it * 8)
            quarter(192, 48, 24)
            inv_rms(3)
            add_normed(1, G_MLP_POST)
            inv_rms(4)
            norm_x(2, G_PLE_PRE)

            U, B = UNIT0["ple"], BLOCK0["ple"]
            for b in range(8):
                for c in range(4):
                    step(0, U + 4 * b + c)
                sum_to(ev[:, b % 2], 0, B + b, ple_summed)
                dve.wait_ge(ple_gate, b + 1)
                dve.tensor_tensor(merged[:, 2 * b:2 * b + 2], ev[:, b % 2], emb[:, 2 * b:2 * b + 2], ALU.mult)\
                   .then_inc(block_done, 1)
            inv_rms(5)
            add_normed(2, G_PLE_POST)

        @block.gpsimd
        def _(pool):
            pool.memset(ones[:, :], 1.0).then_inc(made, 1)
            pool.memset(ident[:, :], 0.0).then_inc(ident_made, 1)
            pool.wait_ge(ident_made, 1)
            pool.affine_select(out=ident[:, :], in_=ident[:, :], compare_op=ALU.not_equal, fill=1.0, base=0,
                               pattern=[[-1, P]], channel_multiplier=1).then_inc(ident_made, 1)

            def add_squares(r):
                for b in range(8):
                    p = 8 * r + b
                    pool.wait_ge(sq_ready, p + 1)
                    if b == 0:
                        if r:
                            pool.wait_ge(sumsq_done, r)
                        pool.tensor_copy(sq_sum[:, :], sq[:, :]).then_inc(sq_added, 1)
                    else:
                        pool.wait_ge(sq_added, p)
                        pool.tensor_tensor(sq_sum[:, :], sq_sum[:, :], sq[:, :], ALU.add).then_inc(sq_added, 1)

            add_squares(0)

            pool.wait_ge(rel_loaded, 16)
            pool.memset(bias_row[:, T:CAUSAL], MASKED)
            starts = bucket_starts()
            for b in range(BUCKETS):
                first, end = T - starts[b + 1], T - starts[b]
                ins = pool.tensor_copy(bias_row[:, first:end], rel[:, b:b + 1].to_broadcast([HEADS, end - first]))
            ins.then_inc(bias_filled, 1)
            pool.wait_ge(bias_filled, 1)
            pool.dma_start(bias_rows.ap(), bias_row[:, :].unsqueeze(1).to_broadcast([HEADS, P, CAUSAL]))\
                .then_inc(bias_stored, 16)
            pool.wait_ge(bias_stored, 16)
            shifted = bass.AP(tensor=bias_rows.ap().tensor, offset=P - 1,
                              ap=[[CAUSAL - 1, P], [P * CAUSAL, HEADS], [1, T]])
            pool.dma_start(bias[:, :, :], shifted).then_inc(bias_loaded, 16)

            pool.wait_ge(block_done, BLOCK0["att"])
            pool.tensor_copy(q_h[:, :], qkv[:, 0, :]).then_inc(head_staged, 1)
            pool.tensor_copy(v_h[:, :], qkv[:, 16, :]).then_inc(head_staged, 1)
            with pool.Fori(1, HEADS) as h:
                pool.wait_ge(scores_done, h)
                pool.tensor_copy(q_h[:, :], qkv[:, ds(h, 1), :]).then_inc(head_staged, 1)
                pool.tensor_copy(v_h[:, :], qkv[:, ds(h + 16, 1), :]).then_inc(head_staged, 1)

            pool.wait_ge(block_done, BLOCK0["xs"])
            pool.memset(mask[:, :], 1.0).then_inc(mask_made, 1)
            pool.wait_ge(mask_made, 1)
            for first, n in ((0, T), (T, P)):
                pool.affine_select(out=mask[:, first:first + n], in_=mask[:, first:first + n],
                                   compare_op=ALU.is_ge, fill=0.0, base=0, pattern=[[1, n]],
                                   channel_multiplier=-1).then_inc(mask_made, 1)

            pool.wait_ge(a_ready, 1)
            pool.dma_start(decay_rows.ap(), a_cum[:, :]).then_inc(a_stored, 16)
            pool.wait_ge(a_stored, 16)
            rows = decay_rows.ap()

            def load_rows(first, half):
                pool.dma_start(a_rows[:, 4 * half:4 * half + 4, :],
                               rows[ds(first + 4 * half, 4), :].partition_broadcast(P))\
                    .then_inc(a_rows_loaded[half], 16)

            load_rows(0, 0)
            load_rows(0, 1)
            with pool.Fori(0, GROUPS - 1) as g:
                for half in range(2):
                    pool.wait_ge(seg_ready, g * 2 + (half + 1))
                    load_rows(g * 8 + 8, half)

            for r in range(1, 6):
                add_squares(r)

        @block.tensor
        def _(pe):
            def products(e, c, act_of, kts, be, bc_, first, last, tiles=2, place=None):
                s, g = c % SLOTS, bc_ % 2
                place = place or (lambda i, t: i * 256 + t * P)
                if first and (bc_ >= 2 or not isinstance(be, int)):
                    pe.wait_ge(block_done, be + (bc_ - 1))
                for i, kt in enumerate(kts):
                    for t in range(tiles):
                        at_ = place(i, t)
                        out_ = bank[2 * g + t]
                        a = act_of(kt)
                        pe.matmul(out_, whi[:, s, at_:at_ + P], a.rearrange("p a t -> p (a t)"),
                                  start=first and i == 0, stop=False)
                        mm = pe.matmul(out_[:, T:2 * T], wlo[:, s, at_:at_ + P], a[:, 0, :],
                                       start=False, stop=last and i == len(kts) - 1)
                return mm

            def unit(e, c, act_of, j, be, bc_, n=BLOCK):
                pe.wait_ge(lo_ready, e + (c + 1))
                products(e, c, act_of, range(4 * j, 4 * j + 4), be, bc_, j == 0, j == n - 1)\
                    .then_inc(unit_done, 1)

            def of(tensor):
                return lambda kt: tensor[:, kt]

            def sum_squares(r):
                pe.wait_ge(sq_added, 8 * (r + 1))
                pe.matmul(bank[4][:, 0:T], ones[:, :], sq_sum[:, 0:T], start=True, stop=False)
                pe.matmul(bank[4][:, 0:T], ones[:, :], sq_sum[:, T:2 * T], start=False, stop=True)\
                  .then_inc(sumsq_done, 1)

            def first_block(c, k, bc_):
                for j in range(4):
                    pe.wait_ge(normed_lo, 8 * k + 2 * j + 2)
                    unit(0, c + j, of(act1), j, 0, bc_)

            pe.wait_ge(made, 1)
            sum_squares(0)

            U, B = UNIT0["qkv"], BLOCK0["qkv"]
            first_block(U, 0, B)
            for j in range(4):
                unit(0, U + 4 + j, of(act1), j, 0, B + 1)
            with pe.Fori(1, 6) as it:
                for c in range(8):
                    unit(it * 8, U + c, of(act1), c % 4, it * 2, B + c // 4)

            U, B = UNIT0["att"], BLOCK0["att"]
            pe.wait_ge(ident_made, 2)
            with pe.Fori(0, 8) as h:
                for c in range(8):
                    unit(h * 8, U + c, of(act1), c % 4, h * 2, B + c // 4)
                    if c == 0:
                        pe.wait_ge(head_staged, h * 2 + 2)
                        pe.matmul(bank[4][:, 0:P], q_h[:, 0:P], qkv[:, ds(h + 8, 1), 0:P].squeeze(1),
                                  start=True, stop=True)
                        pe.matmul(bank[4][:, P:CAUSAL], q_h[:, P:T], qkv[:, ds(h + 8, 1), :].squeeze(1),
                                  start=True, stop=True)
                        for k in range(2):
                            mm = pe.transpose(bank[5][:, k * P:k * P + P], v_h[:, k * P:k * P + P], ident[:, :])
                        mm.then_inc(scores_done, 1)
                    if c == 3:
                        pe.wait_ge(probs_ready, h + 1)
                        for k in range(3):
                            mm = pe.transpose(bank[6][:, k * P:k * P + P], att[:, k * P:k * P + P], ident[:, :])
                        mm.then_inc(probsT_done, 1)
                    if c == 5:
                        pe.wait_ge(v_tok_ready, h + 1)
                        pe.wait_ge(probsT_copied, h + 1)
                        pe.matmul(bank[7][:, 0:T], v_tok[:, 0, :], attT[:, 0:T], start=True, stop=False)
                        pe.matmul(bank[7][:, P:T], v_tok[:, 1, :], attT[:, T:CAUSAL], start=False, stop=True)\
                          .then_inc(pv_done, 1)

            U, B = UNIT0["dt"], BLOCK0["dt"]
            for j in range(2):
                pe.wait_ge(lo_ready, U + j + 1)
                products(0, U + j, of(act1), range(8 * j, 8 * j + 8), 0, B, j == 0, j == 1, tiles=1,
                         place=lambda i, t: i * P).then_inc(unit_done, 1)

            for name, y in (("ga", y_att), ("gc", y_sc)):
                U, B = UNIT0[name], BLOCK0[name]
                with pe.Fori(0, 4) as it:
                    for half in range(2):
                        for j in range(4):
                            unit(it * 12, U + 6 * half + j, of(act1), j, it * 4, B + 2 * half)
                        for j in range(2):
                            unit(it * 12, U + 6 * half + 4 + j, of(y), j, it * 4, B + 2 * half + 1, n=2)

            U, B = UNIT0["xs"], BLOCK0["xs"]
            for c in range(8):
                unit(0, U + c, of(act1), c % 4, 0, B + c // 4)
                if c == 2:
                    pe.wait_ge(bc_ready, 1)
                    for g in range(GROUPS):
                        pe.matmul(bank[4 + g][:, 0:T], bc[:, g, 0:P], bc[:, 4 + g, :], start=True, stop=True)
                        pe.matmul(bank[4 + g][:, T:CAUSAL], bc[:, g, P:T], bc[:, 4 + g, P:T],
                                  start=True, stop=True).then_inc(cb_done, 1)
                if c == 5:
                    pe.wait_ge(a_ready, 1)
                    pe.wait_ge(cb_masked, GROUPS)
                    for i, src in enumerate((dtv, a_cum)):
                        for k in range(2):
                            mm = pe.transpose(bank[4][:, 64 * i + 32 * k:64 * i + 32 * k + 32],
                                              src[:, k * P:k * P + P], ident[0:SSM_HEADS, 0:SSM_HEADS])
                    mm.then_inc(tok_done, 1)

            U, B = UNIT0["ssd"], BLOCK0["ssd"]
            pe.wait_ge(tok_copied, 1)
            with pe.Fori(0, GROUPS) as g:
                for c in range(16):
                    unit(g * 16, U + c, of(act1), c % 4, g * 4, B + c // 4)
                    if c == 4:
                        pe.wait_ge(xs_ready, g + 1)
                        for k in range(2):
                            for t in range(4):
                                mm = pe.transpose(bank[4 + k][:, t * P:t * P + P], xs[:, t, k * P:k * P + P],
                                                  ident[:, :])
                        mm.then_inc(xsT_done, 1)
                    if c in (6, 10):
                        half = c // 10
                        pe.wait_ge(xdt_ready, g + 1)
                        pe.wait_ge(mix_ready, g * 2 + (half + 1))
                        for i in range(4):
                            h = 4 * half + i
                            y = bank[6 + half][HEAD_DIM * (i % 2):HEAD_DIM * (i % 2 + 1), i // 2 * T:i // 2 * T + T]
                            pe.matmul(y, xdt[:, 0, h * HEAD_DIM:(h + 1) * HEAD_DIM], decay[:, i, 0:T],
                                      start=True, stop=False)
                            mm = pe.matmul(y[:, P:T], xdt[:, 1, h * HEAD_DIM:(h + 1) * HEAD_DIM],
                                           decay[:, i, T:CAUSAL], start=False, stop=True)
                        mm.then_inc(y_done, 1)
                    if c == 13:
                        pe.wait_ge(group_squared, g + 1)
                        for t in range(4):
                            mm = pe.matmul(bank[4][:, 0:T], ones[:, :], group_sq[:, t, :],
                                           start=t == 0, stop=t == 3)
                        mm.then_inc(group_summed, 1)

            U, B = UNIT0["gm"], BLOCK0["gm"]
            with pe.Fori(0, 3) as it:
                for c in range(16):
                    unit(it * 16, U + c, of(act2 if c < 8 else act1), c % 4, it * 4, B + c // 4)
            for c in range(8):
                unit(0, U + 48 + c, of(act2), c % 4, 0, B + 12 + c // 4)

            U, B = UNIT0["emb"], BLOCK0["emb"]
            pe.wait_ge(p_split, 1)
            for c in range(4):
                pe.wait_ge(lo_ready, U + c + 1)
                for half in range(2):
                    mm = products(0, U + c, of(p_act), range(2), 0, B + 2 * c + half, True, True,
                                  place=lambda i, t: half * 512 + i * 256 + t * P)
                mm.then_inc(unit_done, 1)

            U, B = UNIT0["out"], BLOCK0["out"]
            with pe.Fori(0, 4) as it:
                for c in range(8):
                    unit(it * 8, U + c, of(act3), c % 4, it * 2, B + c // 4)
            sum_squares(1)
            sum_squares(2)

            U, B = UNIT0["mlp"], BLOCK0["mlp"]

            def blocks(e, c, be, bc_, src, n):
                for i in range(n):
                    for j in range(4):
                        unit(e, c + 4 * i + j, of(src), j, be, bc_ + i)

            first_block(U, 1, B)
            blocks(0, U + 4, 0, B + 1, act1, 1)
            with pe.Fori(0, 3) as it:
                blocks(it * 8, U + 8, it * 2, B + 2, act1, 2)
            with pe.Fori(0, 4) as it:
                blocks(it * 8, U + 32, it * 2, B + 8, act2, 2)
            with pe.Fori(1, 4) as q:
                with pe.Fori(0, 4) as it:
                    blocks(q * 64 + it * 8, U, q * 16 + it * 2, B, act1, 2)
                with pe.Fori(0, 4) as it:
                    blocks(q * 64 + it * 8, U + 32, q * 16 + it * 2, B + 8, act2, 2)
            sum_squares(3)
            sum_squares(4)

            U, B = UNIT0["ple"], BLOCK0["ple"]
            first_block(U, 2, B)
            blocks(0, U + 4, 0, B + 1, act1, 1)
            with pe.Fori(1, 4) as it:
                blocks(it * 8, U, it * 2, B, act1, 2)
            sum_squares(5)


def _blocks(w, c0, c1):
    k = w.shape[0]
    a = w[:, c0:c1].reshape(k // 512, 4, P, (c1 - c0) // 256, 256)
    return a.transpose(3, 0, 2, 1, 4).reshape((c1 - c0) // 256, k // 512, P, 1024)


def _tiles(v):
    return v.reshape(-1, P).T


def kernel(**inputs):
    import concourse.bacc as _bacc
    from concourse.bass_utils import run_bass_kernel_spmd as _run

    a = {k: np.asarray(v) for k, v in inputs.items()}
    w = a["w_in"][0]
    Q, K, V, Z, XBC, DTC, SB, SC, SH, G = 0, 1024, 2048, 3072, 5120, 8192, 8224, 9248, 10272, 11296
    parts = []

    def put(units):
        parts.append(units.reshape(-1, P, 1024))

    put(_blocks(w, Q, Z))
    put(_blocks(w, SC, SH))
    put(_blocks(w, SH, G))
    put(_blocks(w, SB, SC))
    put(_blocks(w, XBC + D, DTC))
    dt = np.concatenate([w[:, DTC:SB], np.zeros((D, P - SSM_HEADS), w.dtype)], axis=1)
    put(dt.reshape(2, 8, P, P).transpose(0, 2, 1, 3))
    for g0, branch in ((G, a["w_br_attn"][0]), (G + 2 * D, a["w_br_conv"][0])):
        gates, branches = _blocks(w, g0, g0 + D), _blocks(branch, 0, D)
        for i in range(8):
            put(gates[i])
            put(branches[i])
    xsb, zb = _blocks(w, XBC, XBC + D), _blocks(w, Z, XBC)
    gates, branches = _blocks(w, G + D, G + 2 * D), _blocks(a["w_br_ssm"][0], 0, D)
    put(xsb[0:2])
    for g in range(GROUPS):
        put(zb[2 * g:2 * g + 2])
        put(xsb[2 * g + 2:2 * g + 4] if g < 3 else gates[0:2])
    for i in range(4):
        put(branches[2 * i:2 * i + 2])
        if i < 3:
            put(gates[2 * i + 2:2 * i + 4])
    put(a["w_ple_proj"][0].reshape(2, P, 4, 2, 256).transpose(2, 1, 3, 0, 4))
    put(_blocks(a["w_out"][0], 0, D))
    up, down = a["w_mlp_up"][0], a["w_mlp_down"][0]
    for q in range(4):
        put(_blocks(up, D * q, D * (q + 1)))
        put(_blocks(down[D * q:D * (q + 1)], 0, D))
    put(_blocks(a["w_ple_gate"][0], 0, D))
    wstream = np.concatenate(parts)
    assert wstream.shape == (UNITS, P, 1024)

    consts = np.concatenate(
        [_tiles(a[n][0]) for n in ("g_mix_pre", "g_mix_post", "g_mlp_pre", "g_mlp_post", "g_ple_pre",
                                   "g_ple_post", "ssm_norm_g")]
        + [_tiles(np.repeat(a["ssm_d"][0], HEAD_DIM)),
           a["ssm_conv_w"][0].reshape(4, 24, P).transpose(2, 1, 0).reshape(P, 96),
           _tiles(a["ssm_conv_b"][0]),
           a["sc_conv_w"][0].reshape(3, 8, P).transpose(2, 1, 0).reshape(P, 24)], axis=1)

    def feature_major(x):
        return x.T.reshape(-1, P, T).transpose(1, 0, 2)

    arrays = {
        "w_stream": wstream,
        "x_in": feature_major(a["x"][0]),
        "p_in": feature_major(a["p"][0, 0]),
        "consts_in": consts,
        "heads_in": np.stack([a["ssm_dt_bias"][0], a["ssm_a_log"][0]], axis=1),
        "rel_in": a["rel_bias"].T,
    }
    arrays = {k: np.ascontiguousarray(v) for k, v in arrays.items()}
    nc = _bacc.Bacc("TRN2", target_bir_lowering=False, num_devices=1, dynamic_dma_scratch_size=8192)
    args = [nc.dram_tensor(k, v.shape, mybir.dt.from_np(v.dtype), kind="ExternalInput").ap()
            for k, v in arrays.items()]
    out = nc.dram_tensor("out", (P, DT, T), F32, kind="ExternalOutput").ap()
    build(nc, *args, out)
    r = _run(nc, [arrays], core_ids=[0])
    y = r.results[0]["out"]
    return y.transpose(2, 1, 0).reshape(1, T, D)
```

```python
from contextlib import ExitStack

import numpy as np

import concourse.bass as bass
from concourse import mybir

F32 = mybir.dt.float32
F32R = mybir.dt.float32r
ALU = mybir.AluOpType
ACT = mybir.ActivationFunctionType
AX = mybir.AxisListType
ds = bass.ds

P = 128
T = 256
D = 2048
DT = D // P
HEADS, BUCKETS = 8, 32
GROUPS, GROUP_HEADS, HEAD_DIM = 4, 8, 64
SSM_HEADS = GROUPS * GROUP_HEADS
EPS = 1e-6
MASKED = -1e30
CAUSAL = T + P

SLOTS = 4
LEAD = SLOTS - 1
BLOCK = 4

STAGES = [
    ("qkv", 48, 12),
    ("att", 64, 16),
    ("dt", 2, 1),
    ("ga", 48, 16),
    ("gc", 48, 16),
    ("xs", 8, 2),
    ("ssd", 64, 16),
    ("gm", 56, 14),
    ("out", 32, 8),
    ("emb0", 1, 2),
    ("emb1", 1, 2),
    ("mlp", 256, 64),
    ("emb2", 1, 2),
    ("emb3", 1, 2),
    ("ple", 32, 8),
]
UNIT0, BLOCK0 = {}, {}
_u = _b = 0
for _name, _units, _blocks in STAGES:
    UNIT0[_name], BLOCK0[_name] = _u, _b
    _u, _b = _u + _units, _b + _blocks
UNITS = _u

G_MIX_PRE, G_MIX_POST, G_MLP_PRE, G_MLP_POST, G_PLE_PRE, G_PLE_POST, G_SSM, D_SKIP = (
    DT * i for i in range(8))
CONV_W = 8 * DT
CONV_B = CONV_W + 24 * 4
SC_W = CONV_B + 24
CONSTS = SC_W + 8 * 3


def bucket_starts():
    n = np.arange(T)
    nf = np.maximum(n, 1).astype(np.float32)
    half = BUCKETS // 2
    large = half + (np.log(nf / np.float32(half)) / np.float32(np.log(128 / half))
                    * np.float32(BUCKETS - half)).astype(np.int32)
    bucket = np.where(n < half, n, np.minimum(large, BUCKETS - 1))
    return [int(np.searchsorted(bucket, b)) for b in range(BUCKETS)] + [T]


def build(nc, wstream, x_in, p_in, consts_in, heads_in, rel_in, out):
    bias_rows = nc.dram_tensor("bias_rows", [HEADS, P, CAUSAL], F32)
    decay_rows = nc.dram_tensor("decay_rows", [SSM_HEADS, T], F32)

    at = [(nc.sbuf_base + 63) // 64 * 64]

    def place(name, shape, dt=F32, where=None):
        size = 4 * int(np.prod(shape[1:]))
        if where is None:
            where = at[0]
            at[0] += (size + 31) // 32 * 32
        return nc.alloc_sbuf_tensor_at(name, shape, dt, offset=where)

    def region(kib):
        where = at[0]
        at[0] += kib * 1024
        return where

    raw = place("w_raw", [P, SLOTS, 1024])
    whi = place("w_hi", [P, SLOTS, 1024], F32R)
    wlo = place("w_lo", [P, SLOTS, 1024], F32R)
    xT = place("x_T", [P, DT, T])
    act1 = place("act1", [P, DT, 2, T], F32R)
    right = place("right", [P, 2, 2, T])
    ev = place("ev", [P, 2, 2, T])
    squares = region(4)
    sq = place("sq", [P, 2 * T], where=squares)
    sq_sum = place("sq_sum", [P, 2 * T], where=squares + 2048)
    group_sq = place("group_sq", [P, 4, T], where=squares)
    pieces = (sq_sum, sq)
    rs = place("rs", [P, T])
    rg = place("rg", [P, T])
    consts = place("consts", [P, CONSTS])
    ident = place("ident", [P, P])
    ones = place("ones", [P, P])
    pT = place("p_T", [P, 2, T])
    p_act = place("p_act", [P, 2, 2, T], F32R)
    dt_raw = place("dt_raw", [SSM_HEADS, T])
    head_consts = place("head_consts", [SSM_HEADS, 2])
    w1 = region(16)
    merged = place("merged", [P, DT, T], where=w1)
    bias = place("bias", [P, HEADS, T], where=w1)
    att = place("att", [P, CAUSAL], where=w1 + 8192)
    attT = place("att_T", [P, CAUSAL], where=w1 + 9728)
    q_h = place("q_h", [P, T], where=w1 + 11264)
    v_h = place("v_h", [P, T], where=w1 + 12288)
    v_tok = place("v_tok", [P, 2, P], where=w1 + 13312)
    negmax = place("negmax", [P, 2], where=w1 + 14336)
    denom = place("denom", [P, 2], where=w1 + 14368)
    w2 = region(32)
    x_sq = place("x_sq", [P, 8, 2 * T], where=w2)
    qkv = place("qkv", [P, 24, T], where=w2)
    y_sc = place("y_sc", [P, 8, 2, T], F32R, where=w2)
    act2 = place("act2", [P, DT, 2, T], F32R, where=w2)
    w3 = region(48)
    y_att = place("y_att", [P, 8, 2, T], F32R, where=w3)
    conv = place("conv", [P, 32, T], where=w3 + 16384)
    bc = place("bc", [P, 8, T], where=w3 + 16384)
    cb = place("cb", [P, GROUPS, CAUSAL], where=w3)
    a_rows = place("a_rows", [P, GROUP_HEADS, T], where=w3 + 6144)
    dtv = place("dt", [SSM_HEADS, T], where=w3 + 14336)
    a_cum = place("a_cum", [SSM_HEADS, T], where=w3 + 15360)
    t0 = w3 + 16384 + 8192
    decay = [place("decay0", [P, 4, CAUSAL], where=t0), place("decay1", [P, 4, CAUSAL], where=w2 + 24576)]
    xs = place("xs", [P, 4, T], where=t0 + 6144)
    z = place("z", [P, 4, T], where=t0 + 10240)
    xdt = place("xdt", [P, 2, 512], where=t0 + 14336)
    mask = place("mask", [P, CAUSAL], where=t0 + 18432)
    dt_tok = place("dt_tok", [P, 2, SSM_HEADS], where=t0 + 19968)
    a_tok = place("a_tok", [P, 2, SSM_HEADS], where=t0 + 20224)
    s_abs = place("s_abs", [SSM_HEADS, T], where=t0)
    s_exp = place("s_exp", [SSM_HEADS, T], where=t0 + 1024)
    s_log = place("s_log", [SSM_HEADS, T], where=t0 + 2048)
    s_dif = place("s_dif", [SSM_HEADS, T], where=t0 + 3072)
    s_one = place("s_one", [SSM_HEADS, T], where=t0 + 4096)
    s_a = place("s_a", [SSM_HEADS, T], where=t0 + 5120)
    ah = place("ah", [SSM_HEADS, 1], where=t0 + 20480)
    act3 = place("act3", [P, DT, 2, T], F32R, where=w3)
    emb = place("emb", [P, DT, T], where=w3 + 32768)
    rel = place("rel", [HEADS, BUCKETS], where=w3)
    bias_row = place("bias_row", [HEADS, CAUSAL], where=w3 + 1024)
    assert at[0] <= nc.sbuf_usable_end, at[0]

    ctx = ExitStack()
    with ctx:
        def sem(name):
            return ctx.enter_context(nc.semaphore(name))

        ps = ctx.enter_context(nc.psum_tensor("ps", [P, 8, 512], F32))
        pair = [ps[:, 2 * g:2 * g + 2, :] for g in range(2)]
        bank = [ps[:, i, :] for i in range(8)]

        w_loaded = [sem(f"w_loaded{s}") for s in range(SLOTS)]
        hi_ready, lo_ready, unit_done = sem("hi_ready"), sem("lo_ready"), sem("unit_done")
        right_copied, block_done = sem("right_copied"), sem("block_done")
        x_loaded = [sem(f"x_loaded{i}") for i in range(4)]
        p_loaded, consts_loaded = sem("p_loaded"), sem("consts_loaded")
        heads_loaded, rel_loaded = sem("heads_loaded"), sem("rel_loaded")
        made, ident_made, mask_made = sem("made"), sem("ident_made"), sem("mask_made")
        bias_filled, bias_stored, bias_loaded = sem("bias_filled"), sem("bias_stored"), sem("bias_loaded")
        x_squared, x_sq_added, x_summed = sem("x_squared"), sem("x_sq_added"), sem("x_summed")
        sq_ready, sq_added, pooled_summed = sem("sq_ready"), sem("sq_added"), sem("pooled_summed")
        piece_ready, piece_summed = sem("piece_ready"), sem("piece_summed")
        var_ready, std_ready, rs_ready = sem("var_ready"), sem("std_ready"), sem("rs_ready")
        normed, normed_hi, normed_lo = sem("normed"), sem("normed_hi"), sem("normed_lo")
        o_normed = sem("o_normed")
        x_updated, x_updated_pool = sem("x_updated"), sem("x_updated_pool")
        head_staged, scores_done = sem("head_staged"), sem("scores_done")
        logits_ready, negmax_ready, exp_ready = sem("logits_ready"), sem("negmax_ready"), sem("exp_ready")
        denom_inv, probs_ready, probsT_done = sem("denom_inv"), sem("probs_ready"), sem("probsT_done")
        probsT_copied, v_tok_ready = sem("probsT_copied"), sem("v_tok_ready")
        pv_done, y_att_hi = sem("pv_done"), sem("y_att_hi")
        sc_product, sc_taps, sc_gated, sc_hi = sem("sc_product"), sem("sc_taps"), sem("sc_gated"), sem("sc_hi")
        gate_ready, branch_summed, branch_gated = sem("gate_ready"), sem("branch_summed"), sem("branch_gated")
        merged_hi = sem("merged_hi")
        dt_summed, bc_taps, bc_ready, cb_done, cb_masked = (
            sem("dt_summed"), sem("bc_taps"), sem("bc_ready"), sem("cb_done"), sem("cb_masked"))
        soft_dve, soft_act = sem("soft_dve"), sem("soft_act")
        a_ready, a_stored, tok_done, tok_copied = sem("a_ready"), sem("a_stored"), sem("tok_done"), sem("tok_copied")
        a_rows_loaded = [sem("a_rows_loaded0"), sem("a_rows_loaded1")]
        seg_ready, decay_ready = sem("seg_ready"), sem("decay_ready")
        mix_ready = [sem("mix_ready0"), sem("mix_ready1")]
        xs_taps, xs_ready, xsT_done, xdt_ready = sem("xs_taps"), sem("xs_ready"), sem("xsT_done"), sem("xdt_ready")
        y_done, z_ready, y_skipped, y_gated = sem("y_done"), sem("z_ready"), sem("y_skipped"), sem("y_gated")
        group_squared, group_added, group_summed = (
            sem("group_squared"), sem("group_added"), sem("group_summed"))
        group_var, group_std_ready, group_rs = sem("group_var"), sem("group_std_ready"), sem("group_rs")
        y_normed, y_ssm_hi, y_ssm_lo = sem("y_normed"), sem("y_ssm_hi"), sem("y_ssm_lo")
        p_hi, p_split = sem("p_hi"), sem("p_split")
        up_summed, hidden_hi, down_summed = sem("up_summed"), sem("hidden_hi"), sem("down_summed")
        merged_zero, ple_summed, ple_gate, out_stored = (
            sem("merged_zero"), sem("ple_summed"), sem("ple_gate"), sem("out_stored"))

        block = ctx.enter_context(nc.Block())

        def two(tensor, i):
            return tensor[:, ds(2 * i, 2)]

        ON_POOL = (1, 3, 5)

        def wait_x(eng, k, b):
            if b in ON_POOL:
                eng.wait_ge(x_updated_pool, len(ON_POOL) * k + ON_POOL.index(b) + 1)
            else:
                own = [i for i in range(8) if i not in ON_POOL]
                eng.wait_ge(x_updated, len(own) * k + own.index(b) + 1)


        @block.sync
        def _(sp):
            for i in range(4):
                sp.dma_start(xT[:, 4 * i:4 * i + 4, :], x_in[:, 4 * i:4 * i + 4, :]).then_inc(x_loaded[i], 16)
            for n in range(SLOTS):
                sp.dma_start(raw[:, n, :], wstream[n]).then_inc(w_loaded[n], 16)
            with sp.Fori(1, UNITS // SLOTS) as it:
                for s in range(SLOTS):
                    sp.wait_ge(lo_ready, it * SLOTS + (s + 1 - SLOTS))
                    sp.dma_start(raw[:, s, :], wstream[ds(it * SLOTS + s, 1)]
                                 .rearrange("o p n -> (o p) n")).then_inc(w_loaded[s], 16)
            for n in range(UNITS // SLOTS * SLOTS, UNITS):
                sp.wait_ge(lo_ready, n + 1 - SLOTS)
                sp.dma_start(raw[:, n % SLOTS, :], wstream[n]).then_inc(w_loaded[n % SLOTS], 16)
            for b in range(8):
                wait_x(sp, 2, b)
                sp.dma_start(out[:, 2 * b:2 * b + 2], xT[:, 2 * b:2 * b + 2]).then_inc(out_stored, 16)
            sp.wait_ge(out_stored, 8 * 16)

        @block.scalar
        def _(act):
            def split_hi(e, c):
                s = c % SLOTS
                act.wait_ge(w_loaded[s], e * 4 + 16 * (c // SLOTS + 1))
                if c >= SLOTS or not isinstance(e, int):
                    act.wait_ge(unit_done, e + (c + 1 - SLOTS))
                act.activation(whi[:, s, :], raw[:, s, :], ACT.Copy).then_inc(hi_ready, 1)

            def step(e, c):
                if isinstance(e, int) and e + c + LEAD >= UNITS:
                    return
                split_hi(e, c + LEAD)

            def copy_right(ue, uc, be, bc_):
                g = bc_ % 2
                act.wait_ge(unit_done, ue + (uc + 1))
                if bc_ >= 2 or not isinstance(be, int):
                    act.wait_ge(block_done, be + (bc_ - 1))
                act.activation(right[:, g], pair[g][:, :, T:2 * T], ACT.Copy).then_inc(right_copied, 1)

            def square(k, b, src):
                if b:
                    act.wait_ge(sq_added, 7 * k + b)
                elif k:
                    act.wait_ge(piece_summed, 8 * k)
                act.activation(sq[:, :], src, ACT.Square).then_inc(sq_ready, 1)

            def square_piece(k, b):
                if b >= 2:
                    act.wait_ge(piece_summed, 8 * (k - 1) + b - 1)
                else:
                    act.wait_ge(pooled_summed, k)
                act.activation(pieces[b % 2][:, :], xT[:, 2 * b:2 * b + 2], ACT.Square).then_inc(piece_ready, 1)

            def std(r):
                act.wait_ge(var_ready, r + 1)
                act.activation(rs[:, :], rs[:, :], ACT.Sqrt).then_inc(std_ready, 1)

            def split_normed(k, j):
                for b in (2 * j, 2 * j + 1):
                    act.wait_ge(normed, 8 * k + b + 1)
                    act.activation(act1[:, 2 * b:2 * b + 2, 0, :], ev[:, b % 2], ACT.Copy)\
                       .then_inc(normed_hi, 1)

            def first_pair(k, U, B, finish=None):
                for c in range(8):
                    if c < 4:
                        split_normed(k, c)
                    step(0, U + c)
                    if c >= 6:
                        copy_right(0, U + c, 0, B + c - 6)
                        if finish:
                            finish(c - 6)

            def sigmoid_gate(slot, be, bc_):
                act.wait_ge(block_done, be + (bc_ + 1))
                act.activation(ev[:, slot], ev[:, slot], ACT.Sigmoid).then_inc(gate_ready, 1)

            act.dma_start(rel[:, :], rel_in).then_inc(rel_loaded, 16)
            act.dma_start(consts[:, :], consts_in).then_inc(consts_loaded, 16)
            act.wait_ge(made, 1)
            act.activation(rg[:, 0:1], ones[:, 0:1], ACT.Sqrt)
            for b in range(8):
                act.wait_ge(x_loaded[b // 2], 16)
                act.activation(x_sq[:, b, :], xT[:, 2 * b:2 * b + 2], ACT.Square).then_inc(x_squared, 1)
            split_hi(0, 0)
            std(0)
            split_hi(0, 1)
            split_hi(0, 2)

            first_pair(0, UNIT0["qkv"], BLOCK0["qkv"])
            with act.Fori(1, 6) as it:
                for c in range(8):
                    step(it * 8, c)
                    if c % 4 == 3:
                        copy_right(it * 8, c, it * 2, c // 4)

            U, B = UNIT0["att"], BLOCK0["att"]
            with act.Fori(0, 8) as h:
                for c in range(8):
                    step(h * 8, U + c)
                    if c == 0:
                        act.wait_ge(scores_done, h + 1)
                        act.activation(v_tok[:, :, :], bank[5][:, 0:T].rearrange("p (k d) -> p k d", k=2),
                                       ACT.Copy).then_inc(v_tok_ready, 1)
                    if c == 1:
                        act.wait_ge(negmax_ready, h + 1)
                        act.activation(att[:, 0:P], att[:, 0:P], ACT.Exp, bias=negmax[:, 0:1],
                                       accum_out=denom[:, 0:1])
                        act.activation(att[:, P:CAUSAL], att[:, P:CAUSAL], ACT.Exp, bias=negmax[:, 1:2],
                                       accum_out=denom[:, 1:2]).then_inc(exp_ready, 1)
                    if c == 6:
                        act.wait_ge(pv_done, h + 1)
                        act.activation(y_att[:, ds(h, 1), 0, :], bank[7][:, 0:T], ACT.Copy)\
                           .then_inc(y_att_hi, 1)
                    if c % 4 == 3:
                        copy_right(h * 8, U + c, h * 2, B + c // 4)

            U, B = UNIT0["dt"], BLOCK0["dt"]
            step(0, U)
            step(0, U + 1)
            act.wait_ge(unit_done, U + 2)
            act.wait_ge(block_done, B - 1)
            act.activation(right[0:SSM_HEADS, B % 2, 0, :], bank[2 * (B % 2)][0:SSM_HEADS, T:2 * T],
                           ACT.Copy).then_inc(right_copied, 1)

            for name in ("ga", "gc"):
                U, B = UNIT0[name], BLOCK0[name]
                with act.Fori(0, 4) as it:
                    for c in range(12):
                        step(it * 12, U + c)
                        if c in (3, 5, 9, 11):
                            copy_right(it * 12, U + c, it * 4, B + (3, 5, 9, 11).index(c))
                        if c in (4, 10):
                            sigmoid_gate(c // 10, it * 4, B + 2 * (c // 10))
                        if c == 7 and name == "ga":
                            act.wait_ge(sc_gated, it + 1)
                            act.activation(y_sc[:, ds(it * 2, 2), 0, :], conv[:, ds(it * 2 + 8, 2), :],
                                           ACT.Copy).then_inc(sc_hi, 1)

            U, B = UNIT0["xs"], BLOCK0["xs"]
            for c in range(8):
                step(0, U + c)
                if c == 0:
                    act.wait_ge(bc_taps, 16)
                    act.activation(bc[:, :, :], bc[:, :, :], ACT.Silu).then_inc(bc_ready, 1)
                if c == 1:
                    act.wait_ge(soft_dve, 1)
                    act.activation(s_exp[:, :], s_abs[:, :], ACT.Exp).then_inc(soft_act, 1)
                    act.activation(ah[:, :], head_consts[:, 1:2], ACT.Exp).then_inc(soft_act, 1)
                    act.wait_ge(soft_dve, 2)
                    act.activation(s_log[:, :], s_one[:, :], ACT.Ln).then_inc(soft_act, 1)
                if c % 4 == 3:
                    copy_right(0, U + c, 0, B + c // 4)

            U, B = UNIT0["ssd"], BLOCK0["ssd"]

            def group_std(g):
                act.wait_ge(group_var, g + 1)
                act.activation(rg[:, :], rg[:, :], ACT.Sqrt).then_inc(group_std_ready, 1)

            def group_hi(g):
                act.wait_ge(y_normed, g + 1)
                act.activation(act2[:, ds(g * 4, 4), 0, :], z[:, :, :], ACT.Copy).then_inc(y_ssm_hi, 1)

            def group(g, first):
                for c in range(16):
                    step(g * 16, U + c)
                    if c == 1 and not first:
                        group_std(g - 1)
                    if c in (7, 9):
                        half = c // 9
                        act.wait_ge(seg_ready, g * 2 + (half + 1))
                        act.activation(decay[half][:, :, :], decay[half][:, :, :], ACT.Exp)\
                           .then_inc(decay_ready, 1)
                    if c == 3 and not first:
                        group_hi(g - 1)
                    if c % 4 == 3:
                        copy_right(g * 16, U + c, g * 4, B + c // 4)
                    if c == 6:
                        act.wait_ge(xs_taps, g * 4 + 4)
                        act.activation(xs[:, :, :], xs[:, :, :], ACT.Silu).then_inc(xs_ready, 1)
                    if c == 12:
                        act.wait_ge(block_done, g * 4 + (B + 2))
                        act.activation(z[:, :, :], z[:, :, :], ACT.Silu).then_inc(z_ready, 1)
                    if c == 15:
                        act.wait_ge(y_gated, g + 1)
                        act.activation(group_sq[:, :, :], z[:, :, :], ACT.Square).then_inc(group_squared, 1)

            group(0, True)
            with act.Fori(1, GROUPS) as g:
                group(g, False)

            U, B = UNIT0["gm"], BLOCK0["gm"]

            def split_merged(e, u, be, bc_):
                act.wait_ge(block_done, be + (bc_ + 1))
                act.activation(act3[:, ds(e + 2 * u, 2), 0, :], merged[:, ds(e + 2 * u, 2), :], ACT.Copy)\
                   .then_inc(merged_hi, 1)

            def branch_pair(ue, uc, be, bc_, e, first=False):
                ends = (6, 7) if first else (3, 7)
                for c in range(8):
                    step(ue, uc + c)
                    if first and c == 1:
                        group_std(GROUPS - 1)
                    if first and c == 3:
                        group_hi(GROUPS - 1)
                    if c in ends:
                        u = ends.index(c)
                        copy_right(ue, uc + c, be, bc_ + u)
                        split_merged(e, u, be, bc_ + u)

            def branches_gates(it, first=False):
                branch_pair(it * 16, U, it * 4, B, it * 4, first)
                for c in range(8, 16):
                    step(it * 16, U + c)
                    if c % 4 == 3:
                        copy_right(it * 16, U + c, it * 4, B + c // 4)
                    if c == 12:
                        sigmoid_gate(0, it * 4, B + 2)
                sigmoid_gate(1, it * 4, B + 3)

            for slot in range(2):
                sigmoid_gate(slot, 0, B - 2 + slot)
            branches_gates(0, first=True)
            with act.Fori(1, 3) as it:
                branches_gates(it)
            branch_pair(0, U + 48, 0, B + 12, 12)

            act.wait_ge(p_loaded, 16)
            act.activation(p_act[:, :, 0, :], pT[:, :, :], ACT.Copy).then_inc(p_hi, 1)

            def emb_unit(i):
                U, B = UNIT0[f"emb{i}"], BLOCK0[f"emb{i}"]
                step(0, U)
                copy_right(0, U, 0, B)
                copy_right(0, U, 0, B + 1)

            U, B = UNIT0["out"], BLOCK0["out"]
            for b in range(8):
                for c in range(4):
                    step(0, U + 4 * b + c)
                copy_right(0, U + 4 * b + 3, 0, B + b)
                act.wait_ge(block_done, B + b + 1)
                square(0, b, merged[:, 2 * b:2 * b + 2])
            emb_unit(0)
            std(1)
            emb_unit(1)
            for b in range(8):
                wait_x(act, 0, b)
                square_piece(1, b)
            std(2)

            def hidden(be, b):
                act.wait_ge(block_done, be + (BLOCK0["mlp"] + b + 1))
                act.activation(act2[:, 2 * b:2 * b + 2, 0, :], ev[:, b % 2], ACT.Copy).then_inc(hidden_hi, 1)

            def quarter(e, be, first=False, last=False):
                if first:
                    first_pair(1, UNIT0["mlp"], BLOCK0["mlp"], lambda b: hidden(0, b))
                for b in range(2 * first, 8):
                    for c in range(4):
                        step(e, UNIT0["mlp"] + 4 * b + c)
                    copy_right(e, UNIT0["mlp"] + 4 * b + 3, be, BLOCK0["mlp"] + b)
                    hidden(be, b)
                for b in range(8, 16):
                    for c in range(4):
                        step(e, UNIT0["mlp"] + 4 * b + c)
                    copy_right(e, UNIT0["mlp"] + 4 * b + 3, be, BLOCK0["mlp"] + b)
                    if last:
                        act.wait_ge(block_done, be + BLOCK0["mlp"] + b + 1)
                        square(1, b - 8, merged[:, 2 * (b - 8):2 * (b - 8) + 2])

            quarter(0, 0, first=True)
            with act.Fori(1, 3) as it:
                quarter(it * 64, it * 16)
            quarter(192, 48, last=True)
            emb_unit(2)
            std(3)
            emb_unit(3)
            for b in range(8):
                wait_x(act, 1, b)
                square_piece(2, b)
            std(4)

            U, B = UNIT0["ple"], BLOCK0["ple"]

            def gated(b):
                act.wait_ge(ple_summed, b + 1)
                act.activation(ev[:, b % 2], ev[:, b % 2], ACT.Sigmoid).then_inc(ple_gate, 1)
                act.wait_ge(block_done, B + b + 1)
                square(2, b, merged[:, 2 * b:2 * b + 2])

            first_pair(2, U, B, gated)
            for b in range(2, 8):
                for c in range(4):
                    step(0, U + 4 * b + c)
                copy_right(0, U + 4 * b + 3, 0, B + b)
                gated(b)
            std(5)

        @block.vector
        def _(dve):
            def split_lo(e, c):
                s = c % SLOTS
                dve.wait_ge(hi_ready, e + (c + 1))
                dve.tensor_tensor(wlo[:, s, :], raw[:, s, :], whi[:, s, :], ALU.subtract)\
                   .then_inc(lo_ready, 1)

            def step(e, c):
                if isinstance(e, int) and e + c + LEAD >= UNITS:
                    return
                split_lo(e, c + LEAD)

            def sum_to(dst, be, bc_, signal):
                g = bc_ % 2
                dve.wait_ge(right_copied, be + (bc_ + 1))
                dve.tensor_tensor(dst, pair[g][:, :, 0:T], right[:, g], ALU.add).then_inc(signal, 1)

            def column(i):
                return consts[:, ds(i, 1)]

            def variance(r):
                if r == 0:
                    dve.wait_ge(x_summed, 1)
                elif r % 2 == 0:
                    dve.wait_ge(piece_summed, 4 * r)
                else:
                    dve.wait_ge(pooled_summed, r // 2 + 1)
                dve.tensor_scalar(rs[:, :], bank[4][:, 0:T], 1.0 / D, EPS, ALU.mult, ALU.add)\
                   .then_inc(var_ready, 1)

            def inverse(r):
                dve.wait_ge(std_ready, r + 1)
                dve.reciprocal(rs[:, :], rs[:, :]).then_inc(rs_ready, 1)
                dve.wait_ge(rs_ready, r + 1)

            def norm_x(k, gain, j):
                for b in (2 * j, 2 * j + 1):
                    if b >= 2:
                        dve.wait_ge(normed_lo, 8 * k + b - 1)
                    for t in range(2):
                        i = dve.scalar_tensor_tensor(
                            ev[:, b % 2, t, :], xT[:, 2 * b + t, :],
                            consts[:, gain + 2 * b + t:gain + 2 * b + t + 1], rs[:, :], ALU.mult, ALU.mult)
                    i.then_inc(normed, 1)
                for b in (2 * j, 2 * j + 1):
                    dve.wait_ge(normed_hi, 8 * k + b + 1)
                    dve.tensor_tensor(act1[:, 2 * b:2 * b + 2, 1, :], ev[:, b % 2],
                                      act1[:, 2 * b:2 * b + 2, 0, :], ALU.subtract).then_inc(normed_lo, 1)

            def first_pair(k, gain, U, finish):
                for c in range(8):
                    if c < 4:
                        norm_x(k, gain, c)
                    if k == 0 and c == 0:
                        split_lo(0, 1)
                        split_lo(0, 2)
                    step(0, U + c)
                    if c >= 6:
                        if c == 6:
                            dve.wait_ge(normed_lo, 8 * k + 8)
                        finish(c - 6)

            def add_normed(k, gain):
                for b in range(8):
                    for t in range(2):
                        i = dve.scalar_tensor_tensor(
                            merged[:, 2 * b + t, :], merged[:, 2 * b + t, :],
                            consts[:, gain + 2 * b + t:gain + 2 * b + t + 1], rs[:, :], ALU.mult, ALU.mult)
                    i.then_inc(o_normed, 1)
                    if b not in ON_POOL:
                        dve.wait_ge(o_normed, 8 * k + b + 1)
                        dve.tensor_tensor(xT[:, 2 * b:2 * b + 2], xT[:, 2 * b:2 * b + 2],
                                          merged[:, 2 * b:2 * b + 2], ALU.add).then_inc(x_updated, 1)

            dve.wait_ge(x_squared, 2)
            dve.tensor_tensor(x_sq[:, 0, :], x_sq[:, 0, :], x_sq[:, 1, :], ALU.add).then_inc(x_sq_added, 1)
            for b in range(2, 8):
                dve.wait_ge(x_squared, b + 1)
                dve.wait_ge(x_sq_added, b - 1)
                dve.tensor_tensor(x_sq[:, 0, :], x_sq[:, 0, :], x_sq[:, b, :], ALU.add).then_inc(x_sq_added, 1)
            dve.wait_ge(x_sq_added, 7)
            dve.tensor_tensor(x_sq[:, 0, 0:T], x_sq[:, 0, 0:T], x_sq[:, 0, T:2 * T], ALU.add)\
               .then_inc(x_sq_added, 1)
            for i in range(4):
                dve.wait_ge(x_loaded[i], 16)
            dve.wait_ge(consts_loaded, 16)
            split_lo(0, 0)
            variance(0)
            inverse(0)

            U, B = UNIT0["qkv"], BLOCK0["qkv"]
            first_pair(0, G_MIX_PRE, U, lambda b: sum_to(qkv[:, 2 * b:2 * b + 2], 0, B + b, block_done))
            with dve.Fori(1, 6) as it:
                for c in range(8):
                    step(it * 8, U + c)
                    if c % 4 == 3:
                        sum_to(qkv[:, ds(it * 4 + 2 * (c // 4), 2), :], it * 2, B + c // 4, block_done)

            U, B = UNIT0["att"], BLOCK0["att"]
            dve.wait_ge(bias_loaded, 16)
            with dve.Fori(0, 8) as h:
                for c in range(8):
                    step(h * 8, U + c)
                    if c == 0:
                        dve.wait_ge(scores_done, h + 1)
                        scale = float(P) ** -0.5
                        dve.scalar_tensor_tensor(att[:, 0:P], bank[4][:, 0:P], scale,
                                                 bias[:, ds(h, 1), P:T], ALU.mult, ALU.add)
                        dve.scalar_tensor_tensor(att[:, P:CAUSAL], bank[4][:, P:CAUSAL], scale,
                                                 bias[:, ds(h, 1), 0:T], ALU.mult, ALU.add)\
                           .then_inc(logits_ready, 1)
                        dve.wait_ge(logits_ready, h + 1)
                        dve.tensor_reduce(negmax[:, 0:1], att[:, 0:P], AX.X, ALU.max, negate=True)
                        dve.tensor_reduce(negmax[:, 1:2], att[:, P:CAUSAL], AX.X, ALU.max, negate=True)\
                           .then_inc(negmax_ready, 1)
                    if c == 2:
                        dve.wait_ge(exp_ready, h + 1)
                        dve.reciprocal(denom[:, :], denom[:, :]).then_inc(denom_inv, 1)
                        dve.wait_ge(denom_inv, h + 1)
                        dve.tensor_scalar(att[:, 0:P], att[:, 0:P], denom[:, 0:1], None, ALU.mult)
                        dve.tensor_scalar(att[:, P:CAUSAL], att[:, P:CAUSAL], denom[:, 1:2], None, ALU.mult)\
                           .then_inc(probs_ready, 1)
                    if c == 4:
                        dve.wait_ge(probsT_done, h + 1)
                        dve.tensor_copy(attT[:, :], bank[6][:, 0:CAUSAL]).then_inc(probsT_copied, 1)
                    if c == 6:
                        dve.wait_ge(y_att_hi, h + 1)
                        dve.tensor_tensor(y_att[:, ds(h, 1), 1, :], bank[7][:, 0:T],
                                          y_att[:, ds(h, 1), 0, :], ALU.subtract)
                    if c % 4 == 3:
                        sum_to(conv[:, ds(h * 4 + 2 * (c // 4), 2), :], h * 2, B + c // 4, block_done)

            U, B = UNIT0["dt"], BLOCK0["dt"]
            step(0, U)
            step(0, U + 1)
            dve.wait_ge(right_copied, B + 1)
            dve.wait_ge(heads_loaded, 16)
            dve.scalar_tensor_tensor(dt_raw[:, :], bank[2 * (B % 2)][0:SSM_HEADS, 0:T], head_consts[:, 0:1],
                                     right[0:SSM_HEADS, B % 2, 0, :], ALU.add, ALU.add).then_inc(block_done, 1)

            def gate_branch(be, bc_, slot, merge, m, first):
                g = bc_ % 2
                sum_to(right[:, g], be, bc_, branch_summed)
                dve.wait_ge(branch_summed, merge)
                dve.wait_ge(gate_ready, merge)
                if first:
                    dve.tensor_tensor(merged[:, ds(m, 2), :], right[:, g], ev[:, slot], ALU.mult)\
                       .then_inc(block_done, 1)
                    return
                dve.tensor_tensor(right[:, g], right[:, g], ev[:, slot], ALU.mult).then_inc(branch_gated, 1)
                dve.wait_ge(branch_gated, merge - 8)
                dve.tensor_tensor(merged[:, ds(m, 2), :], merged[:, ds(m, 2), :], right[:, g], ALU.add)\
                   .then_inc(block_done, 1)

            def sc_step(it, c):
                ch = conv[:, ds(it * 2, 2), :]
                y = conv[:, ds(it * 2 + 8, 2), :]

                def tap(k, shift):
                    for t in range(2):
                        w = column(it * 6 + (SC_W + 3 * t + k))
                        src = conv[:, ds(it * 2 + t, 1), 0:T - shift]
                        dst = conv[:, ds(it * 2 + (8 + t), 1), shift:T]
                        if shift == 0:
                            i = dve.tensor_scalar(dst, src, w, None, ALU.mult)
                        else:
                            i = dve.scalar_tensor_tensor(dst, src, w, dst, ALU.mult, ALU.add)
                    i.then_inc(sc_taps, 1)

                if c == 0:
                    dve.tensor_tensor(ch, ch, y, ALU.mult).then_inc(sc_product, 1)
                if c == 1:
                    dve.wait_ge(sc_product, it + 1)
                    tap(2, 0)
                if c == 2:
                    dve.wait_ge(sc_taps, it * 3 + 1)
                    tap(1, 1)
                if c == 4:
                    dve.wait_ge(sc_taps, it * 3 + 2)
                    tap(0, 2)
                if c == 6:
                    dve.wait_ge(sc_taps, it * 3 + 3)
                    dve.tensor_tensor(y, y, conv[:, ds(it * 2 + 16, 2), :], ALU.mult).then_inc(sc_gated, 1)
                if c == 8:
                    dve.wait_ge(sc_hi, it + 1)
                    dve.tensor_tensor(y_sc[:, ds(it * 2, 2), 1, :], y, y_sc[:, ds(it * 2, 2), 0, :],
                                      ALU.subtract)

            def conv4(src, dst, tile, k, signal):
                shift = 3 - k
                w, b = column(tile * 4 + (CONV_W + k)), column(tile + CONV_B)
                if shift == 0:
                    i = dve.tensor_scalar(dst(0, T), src(0, T), w, b, ALU.mult, ALU.add)
                else:
                    i = dve.scalar_tensor_tensor(dst(shift, T), src(0, T - shift), w, dst(shift, T),
                                                 ALU.mult, ALU.add)
                if signal is not None:
                    i.then_inc(signal, 1)

            def bc_step(it, c):
                if c not in (0, 1, 2, 4):
                    return
                k = {0: 3, 1: 2, 2: 1, 4: 0}[c]
                if c:
                    dve.wait_ge(bc_taps, it * 4 + (3 - k))
                for t in range(2):
                    conv4(lambda a, b: conv[:, ds(it * 2 + (24 + t), 1), a:b],
                          lambda a, b: bc[:, ds(it * 2 + t, 1), a:b], it * 2 + (16 + t), k,
                          bc_taps if t else None)

            for i, (name, side) in enumerate((("ga", sc_step), ("gc", bc_step))):
                U, B = UNIT0[name], BLOCK0[name]
                with dve.Fori(0, 4) as it:
                    for c in range(12):
                        step(it * 12, U + c)
                        side(it, c)
                        if c in (3, 9):
                            sum_to(ev[:, c // 9], it * 4, B + 2 * (c // 9), block_done)
                        if c in (5, 11):
                            gate_branch(it * 4, B + 1 + 2 * (c // 11), c // 11, it * 2 + (8 * i + c // 11 + 1),
                                        it * 4 + 2 * (c // 11), first=i == 0)

            U, B = UNIT0["xs"], BLOCK0["xs"]
            for c in range(8):
                step(0, U + c)
                if c == 0:
                    dve.scalar_tensor_tensor(s_abs[:, :], dt_raw[:, :], -1.0, dt_raw[:, :], ALU.mult, ALU.min)\
                       .then_inc(soft_dve, 1)
                if c == 1:
                    dve.wait_ge(soft_act, 2)
                    dve.tensor_scalar(s_one[:, :], s_exp[:, :], 1.0, None, ALU.add).then_inc(soft_dve, 1)
                    dve.wait_ge(soft_dve, 2)
                    dve.tensor_scalar(s_dif[:, :], s_one[:, :], -1.0, None, ALU.add).then_inc(soft_dve, 1)
                    dve.wait_ge(soft_dve, 3)
                    dve.tensor_scalar(s_a[:, :], s_dif[:, :], 0.0, None, ALU.is_equal).then_inc(soft_dve, 1)
                    dve.wait_ge(soft_dve, 4)
                    dve.tensor_tensor(s_dif[:, :], s_dif[:, :], s_a[:, :], ALU.add).then_inc(soft_dve, 1)
                    dve.wait_ge(soft_act, 3)
                    dve.tensor_tensor(s_log[:, :], s_log[:, :], s_a[:, :], ALU.add).then_inc(soft_dve, 1)
                    dve.wait_ge(soft_dve, 6)
                    dve.reciprocal(s_dif[:, :], s_dif[:, :]).then_inc(soft_dve, 1)
                    dve.tensor_tensor(s_log[:, :], s_log[:, :], s_exp[:, :], ALU.mult).then_inc(soft_dve, 1)
                    dve.wait_ge(soft_dve, 8)
                    dve.tensor_tensor(s_log[:, :], s_log[:, :], s_dif[:, :], ALU.mult).then_inc(soft_dve, 1)
                    dve.wait_ge(soft_dve, 9)
                    dve.scalar_tensor_tensor(dtv[:, :], dt_raw[:, :], 0.0, s_log[:, :], ALU.max, ALU.add)\
                       .then_inc(soft_dve, 1)
                    dve.memset(s_one[:, :], 1.0).then_inc(soft_dve, 1)
                    dve.wait_ge(soft_dve, 11)
                    dve.tensor_scalar(s_a[:, :], dtv[:, :], ah[:, 0:1], -1.0, ALU.mult, ALU.mult)\
                       .then_inc(soft_dve, 1)
                    dve.wait_ge(soft_dve, 12)
                    dve.tensor_tensor_scan(a_cum[:, :], s_one[:, :], s_a[:, :], 0.0, ALU.mult, ALU.add)\
                       .then_inc(a_ready, 1)
                if c == 3:
                    dve.wait_ge(mask_made, 3)
                    for g in range(GROUPS):
                        dve.wait_ge(cb_done, g + 1)
                        dve.tensor_tensor(cb[:, g, :], bank[4 + g][:, 0:CAUSAL], mask[:, :], ALU.mult)\
                           .then_inc(cb_masked, 1)
                if c == 6:
                    dve.wait_ge(tok_done, 1)
                    dve.tensor_copy(dt_tok[:, :, :], bank[4][:, 0:64].rearrange("p (k h) -> p k h", k=2))
                    dve.tensor_copy(a_tok[:, :, :], bank[4][:, 64:128].rearrange("p (k h) -> p k h", k=2))\
                       .then_inc(tok_copied, 1)
                if c % 4 == 3:
                    sum_to(ev[:, c // 4], 0, B + c // 4, block_done)

            U, B = UNIT0["ssd"], BLOCK0["ssd"]
            dve.wait_ge(tok_copied, 1)

            def segments(g, half):
                dve.wait_ge(a_rows_loaded[half], g * 16 + 16)
                for i in range(4):
                    h = 4 * half + i
                    dve.tensor_scalar(decay[half][:, i, 0:T], a_rows[:, h, :], a_tok[:, 0, ds(g * 8 + h, 1)],
                                      0.0, ALU.subtract, ALU.min)
                    ins = dve.tensor_scalar(decay[half][:, i, T:CAUSAL], a_rows[:, h, P:T],
                                            a_tok[:, 1, ds(g * 8 + h, 1)], 0.0, ALU.subtract, ALU.min)
                ins.then_inc(seg_ready, 1)

            def mix_second(g):
                dve.wait_ge(decay_ready, g * 2 + 2)
                dve.tensor_tensor(decay[1][:, :, :], decay[1][:, :, :],
                                  cb[:, ds(g, 1), :].to_broadcast([P, 4, CAUSAL]), ALU.mult)\
                   .then_inc(mix_ready[1], 1)

            def taps(g, k):
                for t in range(4):
                    conv4(lambda a, b: ev[:, t // 2, t % 2, a:b], lambda a, b: xs[:, t, a:b],
                          g * 4 + t, k, xs_taps if t == 3 else None)

            def group_variance(g):
                dve.wait_ge(group_summed, g + 1)
                dve.tensor_scalar(rg[:, :], bank[4][:, 0:T], 1.0 / 512, EPS, ALU.mult, ALU.add)\
                   .then_inc(group_var, 1)

            def group_norm(g):
                dve.wait_ge(group_std_ready, g + 1)
                dve.reciprocal(rg[:, :], rg[:, :]).then_inc(group_rs, 1)
                dve.wait_ge(group_rs, g + 1)
                for t in range(4):
                    ins = dve.scalar_tensor_tensor(z[:, t, :], z[:, t, :], column(g * 4 + (G_SSM + t)),
                                                   rg[:, :], ALU.mult, ALU.mult)
                ins.then_inc(y_normed, 1)

            def group_lo(g):
                dve.wait_ge(y_ssm_hi, g + 1)
                dve.tensor_tensor(act2[:, ds(g * 4, 4), 1, :], z[:, :, :], act2[:, ds(g * 4, 4), 0, :],
                                  ALU.subtract).then_inc(y_ssm_lo, 1)

            def group(g, first):
                for c in range(16):
                    step(g * 16, U + c)
                    if c == 0:
                        dve.wait_ge(block_done, g * 4 + B)
                        dve.wait_ge(lo_ready, g * 16 + (U + 1 + LEAD))
                        taps(g, 3)
                    if c == 1:
                        dve.wait_ge(xs_taps, g * 4 + 1)
                        taps(g, 2)
                        if not first:
                            group_variance(g - 1)
                    if c == 2 and not first:
                        group_norm(g - 1)
                    if c == 3:
                        if first:
                            dve.wait_ge(lo_ready, U + c + 1 + LEAD)
                        else:
                            group_lo(g - 1)
                            dve.wait_ge(y_ssm_lo, g)
                        sum_to(z[:, 0:2, :], g * 4, B, block_done)
                    if c == 4:
                        dve.wait_ge(xs_taps, g * 4 + 2)
                        taps(g, 1)
                    if c == 5:
                        dve.wait_ge(xs_taps, g * 4 + 3)
                        taps(g, 0)
                    if c in (6, 8):
                        segments(g, c // 8)
                    if c == 7:
                        dve.wait_ge(lo_ready, g * 16 + (U + c + 1 + LEAD))
                        sum_to(z[:, 2:4, :], g * 4, B + 1, block_done)
                    if c == 9:
                        dve.wait_ge(xsT_done, g + 1)
                        for k in range(2):
                            ins = dve.tensor_tensor(
                                xdt[:, k, :].rearrange("p (h d) -> p h d", d=HEAD_DIM),
                                bank[4 + k].rearrange("p (h d) -> p h d", d=HEAD_DIM),
                                dt_tok[:, k, ds(g * 8, 8)].unsqueeze(2).to_broadcast([P, 8, HEAD_DIM]),
                                ALU.mult)
                        ins.then_inc(xdt_ready, 1)
                    if c == 11:
                        mix_second(g)
                    if c in (11, 15):
                        sum_to(ev[:, c // 4 - 2], g * 4, B + c // 4, block_done)
                    if c == 14:
                        dve.wait_ge(y_done, g * 2 + 2)
                        for t in range(4):
                            ins = dve.scalar_tensor_tensor(
                                xs[:, t, :], xs[:, t, :], column(g * 4 + (D_SKIP + t)),
                                bank[6 + t // 2][:, t % 2 * T:t % 2 * T + T], ALU.mult, ALU.add)
                        ins.then_inc(y_skipped, 1)
                        dve.wait_ge(y_skipped, g + 1)
                        dve.wait_ge(z_ready, g + 1)
                        dve.tensor_tensor(z[:, :, :], xs[:, :, :], z[:, :, :], ALU.mult).then_inc(y_gated, 1)

            group(0, True)
            with dve.Fori(1, GROUPS) as g:
                group(g, False)

            U, B = UNIT0["gm"], BLOCK0["gm"]

            def branch_pair(ue, uc, be, bc_, e, merge, first=False):
                ends = (6, 7) if first else (3, 7)
                for c in range(8):
                    step(ue, uc + c)
                    if first and c == 1:
                        group_variance(GROUPS - 1)
                    if first and c == 2:
                        group_norm(GROUPS - 1)
                    if first and c == 3:
                        group_lo(GROUPS - 1)
                    if c in ends:
                        u = ends.index(c)
                        gate_branch(be, bc_ + u, u, merge + (u + 1), e + 2 * u, first=False)
                        dve.wait_ge(merged_hi, merge + (u + 1 - 16))
                        dve.tensor_tensor(act3[:, ds(e + 2 * u, 2), 1, :], merged[:, ds(e + 2 * u, 2), :],
                                          act3[:, ds(e + 2 * u, 2), 0, :], ALU.subtract)

            def branches_gates(it, first=False):
                branch_pair(it * 16, U, it * 4, B, it * 4, it * 2 + 16, first)
                for c in range(8, 16):
                    step(it * 16, U + c)
                    if c % 4 == 3:
                        sum_to(ev[:, c // 4 - 2], it * 4, B + c // 4, block_done)

            branches_gates(0, first=True)
            with dve.Fori(1, 3) as it:
                branches_gates(it)
            branch_pair(0, U + 48, 0, B + 12, 12, 22)

            dve.wait_ge(p_hi, 1)
            dve.tensor_tensor(p_act[:, :, 1, :], pT[:, :, :], p_act[:, :, 0, :], ALU.subtract).then_inc(p_split, 1)

            def emb_sums(i):
                for t in range(2):
                    sum_to(emb[:, 4 * i + 2 * t:4 * i + 2 * t + 2], 0, BLOCK0[f"emb{i}"] + t, block_done)

            U, B = UNIT0["out"], BLOCK0["out"]
            for b in range(8):
                for c in range(4):
                    step(0, U + 4 * b + c)
                sum_to(merged[:, 2 * b:2 * b + 2], 0, B + b, block_done)
            step(0, UNIT0["emb0"])
            emb_sums(0)
            variance(1)
            step(0, UNIT0["emb1"])
            inverse(1)
            add_normed(0, G_MIX_POST)
            emb_sums(1)
            variance(2)
            inverse(2)

            def hidden(be, qe, b):
                sum_to(ev[:, b % 2], be, BLOCK0["mlp"] + b, up_summed)
                dve.wait_ge(up_summed, qe + (b + 1))
                dve.scalar_tensor_tensor(ev[:, b % 2], ev[:, b % 2], 0.0, ev[:, b % 2], ALU.max, ALU.mult)\
                   .then_inc(block_done, 1)
                dve.wait_ge(hidden_hi, qe + (b + 1))
                dve.tensor_tensor(act2[:, 2 * b:2 * b + 2, 1, :], ev[:, b % 2],
                                  act2[:, 2 * b:2 * b + 2, 0, :], ALU.subtract)

            def quarter(e, be, qe, first=False):
                if first:
                    first_pair(1, G_MLP_PRE, UNIT0["mlp"], lambda b: hidden(0, 0, b))
                for b in range(2 * first, 8):
                    for c in range(4):
                        step(e, UNIT0["mlp"] + 4 * b + c)
                    hidden(be, qe, b)
                if first:
                    dve.wait_ge(merged_zero, 1)
                for b in range(8, 16):
                    for c in range(4):
                        step(e, UNIT0["mlp"] + 4 * b + c)
                    g = (BLOCK0["mlp"] + b) % 2
                    sum_to(right[:, g], be, BLOCK0["mlp"] + b, down_summed)
                    dve.wait_ge(down_summed, qe + (b - 7))
                    y = merged[:, 2 * (b - 8):2 * (b - 8) + 2]
                    dve.tensor_tensor(y, y, right[:, g], ALU.add).then_inc(block_done, 1)

            quarter(0, 0, 0, first=True)
            with dve.Fori(1, 3) as it:
                quarter(it * 64, it * 16, it * 8)
            quarter(192, 48, 24)
            step(0, UNIT0["emb2"])
            emb_sums(2)
            variance(3)
            step(0, UNIT0["emb3"])
            inverse(3)
            add_normed(1, G_MLP_POST)
            emb_sums(3)
            variance(4)
            inverse(4)

            U, B = UNIT0["ple"], BLOCK0["ple"]

            def gated(b):
                sum_to(ev[:, b % 2], 0, B + b, ple_summed)
                dve.wait_ge(ple_gate, b + 1)
                dve.tensor_tensor(merged[:, 2 * b:2 * b + 2], ev[:, b % 2], emb[:, 2 * b:2 * b + 2], ALU.mult)\
                   .then_inc(block_done, 1)

            first_pair(2, G_PLE_PRE, U, gated)
            for b in range(2, 8):
                for c in range(4):
                    step(0, U + 4 * b + c)
                gated(b)
            variance(5)
            inverse(5)
            add_normed(2, G_PLE_POST)

        @block.gpsimd
        def _(pool):
            pool.memset(ones[:, :], 1.0).then_inc(made, 1)
            pool.memset(ident[:, :], 0.0).then_inc(ident_made, 1)
            pool.wait_ge(ident_made, 1)
            pool.affine_select(out=ident[:, :], in_=ident[:, :], compare_op=ALU.not_equal, fill=1.0, base=0,
                               pattern=[[-1, P]], channel_multiplier=1).then_inc(ident_made, 1)

            pool.dma_start(head_consts[:, :], heads_in).then_inc(heads_loaded, 16)
            pool.dma_start(pT[:, :, :], p_in).then_inc(p_loaded, 16)

            def add_squares(k):
                for b in range(7):
                    pool.wait_ge(sq_ready, 8 * k + b + 1)
                    if b == 0:
                        pool.tensor_copy(sq_sum[:, :], sq[:, :]).then_inc(sq_added, 1)
                    else:
                        pool.wait_ge(sq_added, 7 * k + b)
                        pool.tensor_tensor(sq_sum[:, :], sq_sum[:, :], sq[:, :], ALU.add).then_inc(sq_added, 1)

            pool.wait_ge(rel_loaded, 16)
            pool.memset(bias_row[:, T:CAUSAL], MASKED)
            starts = bucket_starts()
            for b in range(BUCKETS):
                first, end = T - starts[b + 1], T - starts[b]
                ins = pool.tensor_copy(bias_row[:, first:end], rel[:, b:b + 1].to_broadcast([HEADS, end - first]))
            ins.then_inc(bias_filled, 1)
            pool.wait_ge(bias_filled, 1)
            pool.dma_start(bias_rows.ap(), bias_row[:, :].unsqueeze(1).to_broadcast([HEADS, P, CAUSAL]))\
                .then_inc(bias_stored, 16)
            pool.wait_ge(bias_stored, 16)
            shifted = bass.AP(tensor=bias_rows.ap().tensor, offset=P - 1,
                              ap=[[CAUSAL - 1, P], [P * CAUSAL, HEADS], [1, T]])
            pool.dma_start(bias[:, :, :], shifted).then_inc(bias_loaded, 16)

            pool.wait_ge(block_done, BLOCK0["att"])
            pool.tensor_copy(q_h[:, :], qkv[:, 0, :]).then_inc(head_staged, 1)
            pool.tensor_copy(v_h[:, :], qkv[:, 16, :]).then_inc(head_staged, 1)
            with pool.Fori(1, HEADS) as h:
                pool.wait_ge(scores_done, h)
                pool.tensor_copy(q_h[:, :], qkv[:, ds(h, 1), :]).then_inc(head_staged, 1)
                pool.tensor_copy(v_h[:, :], qkv[:, ds(h + 16, 1), :]).then_inc(head_staged, 1)

            pool.wait_ge(block_done, BLOCK0["xs"])
            pool.memset(mask[:, :], 1.0).then_inc(mask_made, 1)
            pool.wait_ge(mask_made, 1)
            for first, n in ((0, T), (T, P)):
                pool.affine_select(out=mask[:, first:first + n], in_=mask[:, first:first + n],
                                   compare_op=ALU.is_ge, fill=0.0, base=0, pattern=[[1, n]],
                                   channel_multiplier=-1).then_inc(mask_made, 1)

            pool.wait_ge(a_ready, 1)
            pool.dma_start(decay_rows.ap(), a_cum[:, :]).then_inc(a_stored, 16)
            pool.wait_ge(a_stored, 16)
            rows = decay_rows.ap()

            def load_rows(first, half):
                pool.dma_start(a_rows[:, 4 * half:4 * half + 4, :],
                               rows[ds(first + 4 * half, 4), :].partition_broadcast(P))\
                    .then_inc(a_rows_loaded[half], 16)

            def mix_first(g):
                pool.wait_ge(decay_ready, g * 2 + 1)
                pool.tensor_tensor(decay[0][:, :, :], decay[0][:, :, :],
                                   cb[:, ds(g, 1), :].to_broadcast([P, 4, CAUSAL]), ALU.mult)\
                    .then_inc(mix_ready[0], 1)

            def add_group(g):
                pool.wait_ge(group_squared, g + 1)
                pool.tensor_tensor(group_sq[:, 0:2, :], group_sq[:, 0:2, :], group_sq[:, 2:4, :], ALU.add)\
                    .then_inc(group_added, 1)
                pool.wait_ge(group_added, g * 2 + 1)
                pool.tensor_tensor(group_sq[:, 0, :], group_sq[:, 0, :], group_sq[:, 1, :], ALU.add)\
                    .then_inc(group_added, 1)

            load_rows(0, 0)
            load_rows(0, 1)
            pool.wait_ge(cb_masked, GROUPS)
            with pool.Fori(0, GROUPS - 1) as g:
                for half in range(2):
                    if half == 0:
                        mix_first(g)
                    pool.wait_ge(seg_ready, g * 2 + (half + 1))
                    load_rows(g * 8 + 8, half)
                add_group(g)
            mix_first(GROUPS - 1)
            add_group(GROUPS - 1)

            for k in range(3):
                add_squares(k)
                for b in ON_POOL:
                    pool.wait_ge(o_normed, 8 * k + b + 1)
                    pool.tensor_tensor(xT[:, 2 * b:2 * b + 2], xT[:, 2 * b:2 * b + 2],
                                       merged[:, 2 * b:2 * b + 2], ALU.add).then_inc(x_updated_pool, 1)
                if k == 0:
                    pool.wait_ge(x_updated, 8 - len(ON_POOL))
                    pool.wait_ge(x_updated_pool, len(ON_POOL))
                    pool.memset(merged[:, :, :], 0.0).then_inc(merged_zero, 1)

        @block.tensor
        def _(pe):
            def products(e, c, act_of, kts, be, bc_, first, last, tiles=2, place=None):
                s, g = c % SLOTS, bc_ % 2
                place = place or (lambda i, t: i * 256 + t * P)
                if first and (bc_ >= 2 or not isinstance(be, int)):
                    pe.wait_ge(block_done, be + (bc_ - 1))
                for i, kt in enumerate(kts):
                    for t in range(tiles):
                        at_ = place(i, t)
                        out_ = bank[2 * g + t]
                        a = act_of(kt)
                        pe.matmul(out_, whi[:, s, at_:at_ + P], a.rearrange("p a t -> p (a t)"),
                                  start=first and i == 0, stop=False)
                        mm = pe.matmul(out_[:, T:2 * T], wlo[:, s, at_:at_ + P], a[:, 0, :],
                                       start=False, stop=last and i == len(kts) - 1)
                return mm

            def unit(e, c, act_of, j, be, bc_, n=BLOCK):
                pe.wait_ge(lo_ready, e + (c + 1))
                products(e, c, act_of, range(4 * j, 4 * j + 4), be, bc_, j == 0, j == n - 1)\
                    .then_inc(unit_done, 1)

            def of(tensor):
                return lambda kt: tensor[:, kt]

            def sum_pair(src, first, last):
                pe.matmul(bank[4][:, 0:T], ones[:, :], src[:, 0:T], start=first, stop=False)
                return pe.matmul(bank[4][:, 0:T], ones[:, :], src[:, T:2 * T], start=False, stop=last)

            def sum_pooled(k):
                pe.wait_ge(sq_added, 7 * k + 7)
                sum_pair(sq_sum, True, False)
                pe.wait_ge(sq_ready, 8 * k + 8)
                sum_pair(sq, False, True).then_inc(pooled_summed, 1)

            def sum_pieces(k):
                for b in range(8):
                    pe.wait_ge(piece_ready, 8 * (k - 1) + b + 1)
                    sum_pair(pieces[b % 2], b == 0, b == 7).then_inc(piece_summed, 1)

            def first_pair(c, k, bc_):
                for i in range(8):
                    j = i // 2
                    pe.wait_ge(normed_lo, 8 * k + 2 * j + 2)
                    unit(0, c + i, of(act1), j, 0, bc_ + i % 2)

            pe.wait_ge(made, 1)
            pe.wait_ge(x_sq_added, 8)
            pe.matmul(bank[4][:, 0:T], ones[:, :], x_sq[:, 0, 0:T], start=True, stop=True).then_inc(x_summed, 1)

            U, B = UNIT0["qkv"], BLOCK0["qkv"]
            first_pair(U, 0, B)
            with pe.Fori(1, 6) as it:
                for c in range(8):
                    unit(it * 8, U + c, of(act1), c % 4, it * 2, B + c // 4)

            U, B = UNIT0["att"], BLOCK0["att"]
            pe.wait_ge(ident_made, 2)
            with pe.Fori(0, 8) as h:
                for c in range(8):
                    unit(h * 8, U + c, of(act1), c % 4, h * 2, B + c // 4)
                    if c == 0:
                        pe.wait_ge(head_staged, h * 2 + 2)
                        pe.matmul(bank[4][:, 0:P], q_h[:, 0:P], qkv[:, ds(h + 8, 1), 0:P].squeeze(1),
                                  start=True, stop=True)
                        pe.matmul(bank[4][:, P:CAUSAL], q_h[:, P:T], qkv[:, ds(h + 8, 1), :].squeeze(1),
                                  start=True, stop=True)
                        for k in range(2):
                            mm = pe.transpose(bank[5][:, k * P:k * P + P], v_h[:, k * P:k * P + P], ident[:, :])
                        mm.then_inc(scores_done, 1)
                    if c == 3:
                        pe.wait_ge(probs_ready, h + 1)
                        for k in range(3):
                            mm = pe.transpose(bank[6][:, k * P:k * P + P], att[:, k * P:k * P + P], ident[:, :])
                        mm.then_inc(probsT_done, 1)
                    if c == 5:
                        pe.wait_ge(v_tok_ready, h + 1)
                        pe.wait_ge(probsT_copied, h + 1)
                        pe.matmul(bank[7][:, 0:T], v_tok[:, 0, :], attT[:, 0:T], start=True, stop=False)
                        pe.matmul(bank[7][:, P:T], v_tok[:, 1, :], attT[:, T:CAUSAL], start=False, stop=True)\
                          .then_inc(pv_done, 1)

            U, B = UNIT0["dt"], BLOCK0["dt"]
            for j in range(2):
                pe.wait_ge(lo_ready, U + j + 1)
                products(0, U + j, of(act1), range(8 * j, 8 * j + 8), 0, B, j == 0, j == 1, tiles=1,
                         place=lambda i, t: i * P).then_inc(unit_done, 1)

            for name, y in (("ga", y_att), ("gc", y_sc)):
                U, B = UNIT0[name], BLOCK0[name]
                with pe.Fori(0, 4) as it:
                    for half in range(2):
                        for j in range(4):
                            unit(it * 12, U + 6 * half + j, of(act1), j, it * 4, B + 2 * half)
                        for j in range(2):
                            unit(it * 12, U + 6 * half + 4 + j, of(y), j, it * 4, B + 2 * half + 1, n=2)

            U, B = UNIT0["xs"], BLOCK0["xs"]
            for c in range(8):
                unit(0, U + c, of(act1), c % 4, 0, B + c // 4)
                if c == 2:
                    pe.wait_ge(bc_ready, 1)
                    for g in range(GROUPS):
                        pe.matmul(bank[4 + g][:, 0:T], bc[:, g, 0:P], bc[:, 4 + g, :], start=True, stop=True)
                        pe.matmul(bank[4 + g][:, T:CAUSAL], bc[:, g, P:T], bc[:, 4 + g, P:T],
                                  start=True, stop=True).then_inc(cb_done, 1)
                if c == 5:
                    pe.wait_ge(a_ready, 1)
                    pe.wait_ge(cb_masked, GROUPS)
                    for i, src in enumerate((dtv, a_cum)):
                        for k in range(2):
                            mm = pe.transpose(bank[4][:, 64 * i + 32 * k:64 * i + 32 * k + 32],
                                              src[:, k * P:k * P + P], ident[0:SSM_HEADS, 0:SSM_HEADS])
                    mm.then_inc(tok_done, 1)

            U, B = UNIT0["ssd"], BLOCK0["ssd"]
            pe.wait_ge(tok_copied, 1)

            def sum_group(g):
                pe.wait_ge(group_added, g * 2 + 2)
                pe.matmul(bank[4][:, 0:T], ones[:, :], group_sq[:, 0, :], start=True, stop=True)\
                  .then_inc(group_summed, 1)

            def group(g, first):
                for c in range(16):
                    unit(g * 16, U + c, of(act1), c % 4, g * 4, B + c // 4)
                    if c == 0 and not first:
                        sum_group(g - 1)
                    if c == 8:
                        pe.wait_ge(xs_ready, g + 1)
                        for k in range(2):
                            for t in range(4):
                                mm = pe.transpose(bank[4 + k][:, t * P:t * P + P], xs[:, t, k * P:k * P + P],
                                                  ident[:, :])
                        mm.then_inc(xsT_done, 1)
                    if c in (11, 13):
                        half = c // 13
                        pe.wait_ge(xdt_ready, g + 1)
                        pe.wait_ge(mix_ready[half], g + 1)
                        for i in range(4):
                            h = 4 * half + i
                            y = bank[6 + half][HEAD_DIM * (i % 2):HEAD_DIM * (i % 2 + 1), i // 2 * T:i // 2 * T + T]
                            pe.matmul(y, xdt[:, 0, h * HEAD_DIM:(h + 1) * HEAD_DIM], decay[half][:, i, 0:T],
                                      start=True, stop=False)
                            mm = pe.matmul(y[:, P:T], xdt[:, 1, h * HEAD_DIM:(h + 1) * HEAD_DIM],
                                           decay[half][:, i, T:CAUSAL], start=False, stop=True)
                        mm.then_inc(y_done, 1)

            group(0, True)
            with pe.Fori(1, GROUPS) as g:
                group(g, False)

            U, B = UNIT0["gm"], BLOCK0["gm"]
            for c in range(8):
                if c == 6:
                    pe.wait_ge(y_ssm_lo, GROUPS)
                unit(0, U + c, of(act2), c // 2, 0, B + c % 2)
                if c == 0:
                    sum_group(GROUPS - 1)
            for c in range(8, 16):
                unit(0, U + c, of(act1), c % 4, 0, B + c // 4)
            with pe.Fori(1, 3) as it:
                for c in range(16):
                    unit(it * 16, U + c, of(act2 if c < 8 else act1), c % 4, it * 4, B + c // 4)
            for c in range(8):
                unit(0, U + 48 + c, of(act2), c % 4, 0, B + 12 + c // 4)

            def emb_unit(i):
                if i == 0:
                    pe.wait_ge(p_split, 1)
                U, B = UNIT0[f"emb{i}"], BLOCK0[f"emb{i}"]
                pe.wait_ge(lo_ready, U + 1)
                for half in range(2):
                    mm = products(0, U, of(p_act), range(2), 0, B + half, True, True,
                                  place=lambda i, t: half * 512 + i * 256 + t * P)
                mm.then_inc(unit_done, 1)

            U, B = UNIT0["out"], BLOCK0["out"]
            with pe.Fori(0, 4) as it:
                for c in range(8):
                    unit(it * 8, U + c, of(act3), c % 4, it * 2, B + c // 4)
            emb_unit(0)
            sum_pooled(0)
            emb_unit(1)
            sum_pieces(1)

            U, B = UNIT0["mlp"], BLOCK0["mlp"]

            def blocks(e, c, be, bc_, src, n):
                for i in range(n):
                    for j in range(4):
                        unit(e, c + 4 * i + j, of(src), j, be, bc_ + i)

            first_pair(U, 1, B)
            with pe.Fori(0, 3) as it:
                blocks(it * 8, U + 8, it * 2, B + 2, act1, 2)
            with pe.Fori(0, 4) as it:
                blocks(it * 8, U + 32, it * 2, B + 8, act2, 2)
            with pe.Fori(1, 4) as q:
                with pe.Fori(0, 4) as it:
                    blocks(q * 64 + it * 8, U, q * 16 + it * 2, B, act1, 2)
                with pe.Fori(0, 4) as it:
                    blocks(q * 64 + it * 8, U + 32, q * 16 + it * 2, B + 8, act2, 2)
            emb_unit(2)
            sum_pooled(1)
            emb_unit(3)
            sum_pieces(2)

            U, B = UNIT0["ple"], BLOCK0["ple"]
            first_pair(U, 2, B)
            with pe.Fori(1, 4) as it:
                blocks(it * 8, U, it * 2, B, act1, 2)
            sum_pooled(2)


def _blocks(w, c0, c1):
    k = w.shape[0]
    a = w[:, c0:c1].reshape(k // 512, 4, P, (c1 - c0) // 256, 256)
    return a.transpose(3, 0, 2, 1, 4).reshape((c1 - c0) // 256, k // 512, P, 1024)


def _in_turns(blocks):
    first = blocks[:2].transpose(1, 0, 2, 3)
    return np.concatenate([first.reshape(-1, P, 1024), blocks[2:].reshape(-1, P, 1024)])


def _tiles(v):
    return v.reshape(-1, P).T


def kernel(**inputs):
    import concourse.bacc as _bacc
    from concourse.bass_utils import run_bass_kernel_spmd as _run

    a = {k: np.asarray(v) for k, v in inputs.items()}
    w = a["w_in"][0]
    Q, K, V, Z, XBC, DTC, SB, SC, SH, G = 0, 1024, 2048, 3072, 5120, 8192, 8224, 9248, 10272, 11296
    parts = []

    def put(units):
        parts.append(units.reshape(-1, P, 1024))

    put(_in_turns(_blocks(w, Q, Z)))
    put(_blocks(w, SC, SH))
    put(_blocks(w, SH, G))
    put(_blocks(w, SB, SC))
    put(_blocks(w, XBC + D, DTC))
    dt = np.concatenate([w[:, DTC:SB], np.zeros((D, P - SSM_HEADS), w.dtype)], axis=1)
    put(dt.reshape(2, 8, P, P).transpose(0, 2, 1, 3))
    for g0, branch in ((G, a["w_br_attn"][0]), (G + 2 * D, a["w_br_conv"][0])):
        gates, branches = _blocks(w, g0, g0 + D), _blocks(branch, 0, D)
        for i in range(8):
            put(gates[i])
            put(branches[i])
    xsb, zb = _blocks(w, XBC, XBC + D), _blocks(w, Z, XBC)
    gates, branches = _blocks(w, G + D, G + 2 * D), _blocks(a["w_br_ssm"][0], 0, D)
    put(xsb[0:2])
    for g in range(GROUPS):
        put(zb[2 * g:2 * g + 2])
        put(xsb[2 * g + 2:2 * g + 4] if g < 3 else gates[0:2])
    for i in range(4):
        put(branches[2 * i:2 * i + 2] if i else _in_turns(branches[:2]))
        if i < 3:
            put(gates[2 * i + 2:2 * i + 4])
    emb = a["w_ple_proj"][0].reshape(2, P, 4, 2, 256).transpose(2, 1, 3, 0, 4)
    outs = _blocks(a["w_out"][0], 0, D)
    put(outs)
    put(emb[:2])
    up, down = a["w_mlp_up"][0], a["w_mlp_down"][0]
    for q in range(4):
        ups = _blocks(up, D * q, D * (q + 1))
        put(ups if q else _in_turns(ups))
        put(_blocks(down[D * q:D * (q + 1)], 0, D))
    put(emb[2:])
    put(_in_turns(_blocks(a["w_ple_gate"][0], 0, D)))
    wstream = np.concatenate(parts)
    assert wstream.shape == (UNITS, P, 1024)

    consts = np.concatenate(
        [_tiles(a[n][0]) for n in ("g_mix_pre", "g_mix_post", "g_mlp_pre", "g_mlp_post", "g_ple_pre",
                                   "g_ple_post", "ssm_norm_g")]
        + [_tiles(np.repeat(a["ssm_d"][0], HEAD_DIM)),
           a["ssm_conv_w"][0].reshape(4, 24, P).transpose(2, 1, 0).reshape(P, 96),
           _tiles(a["ssm_conv_b"][0]),
           a["sc_conv_w"][0].reshape(3, 8, P).transpose(2, 1, 0).reshape(P, 24)], axis=1)

    def feature_major(x):
        return x.T.reshape(-1, P, T).transpose(1, 0, 2)

    arrays = {
        "w_stream": wstream,
        "x_in": feature_major(a["x"][0]),
        "p_in": feature_major(a["p"][0, 0]),
        "consts_in": consts,
        "heads_in": np.stack([a["ssm_dt_bias"][0], a["ssm_a_log"][0]], axis=1),
        "rel_in": a["rel_bias"].T,
    }
    arrays = {k: np.ascontiguousarray(v) for k, v in arrays.items()}
    nc = _bacc.Bacc("TRN2", target_bir_lowering=False, num_devices=1, dynamic_dma_scratch_size=8192)
    args = [nc.dram_tensor(k, v.shape, mybir.dt.from_np(v.dtype), kind="ExternalInput").ap()
            for k, v in arrays.items()]
    out = nc.dram_tensor("out", (P, DT, T), F32, kind="ExternalOutput").ap()
    build(nc, *args, out)
    r = _run(nc, [arrays], core_ids=[0])
    y = r.results[0]["out"]
    return y.transpose(2, 1, 0).reshape(1, T, D)
```
